# Optimizing a Trainium2 kernel written in Bass

```python
import math
import jax, jax.numpy as jnp
from jax import lax
import numpy as np
import jax
import jax.numpy as jnp

D_MODEL = 1024
BATCH = 1
SEQ = 256
DEPTH = 2

N_HEADS = 16
HEAD_DIM = D_MODEL // N_HEADS
Q_BLOCK = 128
POOL_WINDOWS = (2, 4, 8, 16)
N_POOL_GROUPS = len(POOL_WINDOWS)
POOL_CH = D_MODEL // N_POOL_GROUPS
N_EXPERTS = 32
N_EXPERT_GROUPS = 4
EXPERTS_PER_GROUP = N_EXPERTS // N_EXPERT_GROUPS
TOPK_GROUPS = 1
TOP_K = 2
D_FF_EXPERT = D_MODEL // 2
EXPERT_BLOCK = 256
N_MIXERS = 2
N_ATTN = (DEPTH + 1) // 2
N_POOL = DEPTH // 2
RMS_EPS = 1e-6


def rmsnorm(x, g):
    xf = x.astype(jnp.float32)
    xf = xf * lax.rsqrt(jnp.mean(xf * xf, axis=-1, keepdims=True) + RMS_EPS)
    return (xf * g.astype(jnp.float32)).astype(x.dtype)

def modulate(h, shift, scale):
    return h * (1.0 + scale[:, None, :]) + shift[:, None, :]

def fox_attention(h, w_in, f_bias, w_o):
    B, S, D = h.shape
    proj = h @ w_in
    q, k, v, f = jnp.split(proj, [D, 2 * D, 3 * D], axis=-1)
    to_heads = lambda t: t.reshape(B, S, N_HEADS, HEAD_DIM).transpose(0, 2, 1, 3)
    q, k, v = to_heads(q), to_heads(k), to_heads(v)
    log_f = jax.nn.log_sigmoid(f.astype(jnp.float32) + f_bias.astype(jnp.float32))
    F = jnp.cumsum(log_f, axis=1).transpose(0, 2, 1)
    scale = 1.0 / math.sqrt(HEAD_DIM)
    kpos = jnp.arange(S)
    n_blocks = S // Q_BLOCK

    def q_block(i):
        start = i * Q_BLOCK
        qb = lax.dynamic_slice_in_dim(q, start, Q_BLOCK, axis=2)
        Fq = lax.dynamic_slice_in_dim(F, start, Q_BLOCK, axis=2)
        logits = jnp.einsum('bhqd,bhkd->bhqk', qb, k).astype(jnp.float32) * scale
        logits = logits + Fq[..., :, None] - F[:, :, None, :]
        qpos = start + jnp.arange(Q_BLOCK)
        causal = kpos[None, :] <= qpos[:, None]
        logits = jnp.where(causal[None, None], logits, -jnp.inf)
        p = jax.nn.softmax(logits, axis=-1)
        return jnp.einsum('bhqk,bhkd->bhqd', p.astype(v.dtype), v)

    o = lax.map(q_block, jnp.arange(n_blocks))
    o = o.transpose(1, 0, 3, 2, 4).reshape(B, S, D)
    return (o @ w_o).astype(h.dtype)

def pool_mixer(h, w_pool, ch_scale):
    B, S, D = h.shape
    hf = h.astype(jnp.float32)
    cs = jnp.cumsum(hf, axis=1)
    t = jnp.arange(S)
    outs = []
    for g, win in enumerate(POOL_WINDOWS):
        sl = slice(g * POOL_CH, (g + 1) * POOL_CH)
        csg = cs[..., sl]
        shifted = jnp.pad(csg, ((0, 0), (win, 0), (0, 0)))[:, :S]
        count = jnp.minimum(t + 1, win).astype(jnp.float32)[None, :, None]
        outs.append((csg - shifted) / count - hf[..., sl])
    pooled = jnp.stack(outs, axis=2).astype(h.dtype)
    y = jnp.einsum('bsgc,gce->bsge', pooled, w_pool).reshape(B, S, D)
    return (y * ch_scale).astype(h.dtype)

def grouped_moe(h, router_w, router_bias, w1, w3, w2):
    B, S, D = h.shape
    T = B * S
    hf = h.reshape(T, D)
    scores = jax.nn.sigmoid((hf @ router_w).astype(jnp.float32))
    sel = scores + router_bias.astype(jnp.float32)
    sel_g = sel.reshape(T, N_EXPERT_GROUPS, EXPERTS_PER_GROUP)
    group_score = lax.top_k(sel_g, TOP_K)[0].sum(-1)
    _, g_idx = lax.top_k(group_score, TOPK_GROUPS)
    g_mask = jnp.any(g_idx[..., None] == jnp.arange(N_EXPERT_GROUPS), axis=1)
    e_mask = jnp.repeat(g_mask, EXPERTS_PER_GROUP, axis=1)
    _, e_idx = lax.top_k(jnp.where(e_mask, sel, -jnp.inf), TOP_K)
    gate = jnp.take_along_axis(scores, e_idx, axis=1)
    gate = gate / jnp.sum(gate, axis=-1, keepdims=True)

    A = T * TOP_K
    e_flat = e_idx.reshape(A)
    tok_flat = jnp.repeat(jnp.arange(T, dtype=jnp.int32), TOP_K)
    w_flat = gate.reshape(A)
    order = jnp.argsort(e_flat)
    e_sorted = e_flat[order]
    counts = jnp.bincount(e_flat, length=N_EXPERTS)
    padded = ((counts + EXPERT_BLOCK - 1) // EXPERT_BLOCK) * EXPERT_BLOCK
    starts = jnp.cumsum(counts) - counts
    pends = jnp.cumsum(padded)
    pstarts = pends - padded
    rank = jnp.arange(A) - starts[e_sorted]
    dest = pstarts[e_sorted] + rank
    n_blocks = A // EXPERT_BLOCK + N_EXPERTS
    P = n_blocks * EXPERT_BLOCK
    row_tok = jnp.full((P,), T, dtype=jnp.int32).at[dest].set(tok_flat[order])
    row_w = jnp.zeros((P,), jnp.float32).at[dest].set(w_flat[order])
    block_e = jnp.minimum(
        jnp.searchsorted(pends, jnp.arange(n_blocks) * EXPERT_BLOCK, side='right'),
        N_EXPERTS - 1)
    x_rows = jnp.concatenate([hf, jnp.zeros((1, D), hf.dtype)], axis=0)[row_tok]
    x_rows = x_rows.reshape(n_blocks, EXPERT_BLOCK, D)

    def expert_block(args):
        xb, e = args
        return (jax.nn.silu(xb @ w1[e]) * (xb @ w3[e])) @ w2[e]

    y = lax.map(expert_block, (x_rows, block_e)).reshape(P, D)
    out = jax.ops.segment_sum(y.astype(jnp.float32) * row_w[:, None], row_tok,
                              num_segments=T + 1)[:T]
    return out.reshape(B, S, D).astype(h.dtype)

def first_inputs(seed: int = 0) -> dict:
    key = jax.random.key(seed)
    ks = jax.random.split(key, 20)
    D, H, E, Fd = D_MODEL, N_HEADS, N_EXPERTS, D_FF_EXPERT
    nrm = lambda k, shape, s: jax.random.normal(k, shape, jnp.float32) * s
    return {
        "x": nrm(ks[0], (BATCH, SEQ, D), 1.0),
        "c": nrm(ks[1], (BATCH, D), 1.0),
        "norm_mix_g": 1.0 + nrm(ks[2], (DEPTH, D), 0.05),
        "norm_ffn_g": 1.0 + nrm(ks[3], (DEPTH, D), 0.05),
        "ada_w": nrm(ks[4], (DEPTH, D, 6 * D), 0.5 * D ** -0.5),
        "ada_b": nrm(ks[5], (DEPTH, 6 * D), 0.01),
        "attn_w_in": nrm(ks[6], (N_ATTN, D, 3 * D + H), D ** -0.5),
        "attn_f_bias": 2.0 + nrm(ks[7], (N_ATTN, H), 0.5),
        "attn_w_o": nrm(ks[8], (N_ATTN, D, D), D ** -0.5),
        "pool_w": nrm(ks[9], (N_POOL, N_POOL_GROUPS, POOL_CH, POOL_CH), POOL_CH ** -0.5),
        "pool_scale": 0.5 + nrm(ks[10], (N_POOL, D), 0.1),
        "router_w": nrm(ks[11], (D, E), D ** -0.5),
        "router_bias": nrm(ks[12], (E,), 0.01),
        "exp_w1": nrm(ks[13], (DEPTH, E, D, Fd), D ** -0.5),
        "exp_w3": nrm(ks[14], (DEPTH, E, D, Fd), D ** -0.5),
        "exp_w2": nrm(ks[15], (DEPTH, E, Fd, D), Fd ** -0.5),
        "norm_final_g": 1.0 + nrm(ks[16], (D,), 0.05),
    }

def first_block(x, c, norm_mix_g, norm_ffn_g, ada_w, ada_b, attn_w_in, attn_f_bias,
              attn_w_o, pool_w, pool_scale, router_w, router_bias, exp_w1, exp_w3,
              exp_w2, norm_final_g):
    c_act = jax.nn.silu(c)
    for i in range(DEPTH):
        mod = c_act @ ada_w[i] + ada_b[i]
        sh_m, sc_m, gt_m, sh_f, sc_f, gt_f = jnp.split(mod, 6, axis=-1)
        h = modulate(rmsnorm(x, norm_mix_g[i]), sh_m, sc_m)
        if i % N_MIXERS == 0:
            j = i // N_MIXERS
            y = fox_attention(h, attn_w_in[j], attn_f_bias[j], attn_w_o[j])
        else:
            j = i // N_MIXERS
            y = pool_mixer(h, pool_w[j], pool_scale[j])
        x = x + gt_m[:, None, :] * y
        h = modulate(rmsnorm(x, norm_ffn_g[i]), sh_f, sc_f)
        y = grouped_moe(h, router_w, router_bias, exp_w1[i], exp_w3[i], exp_w2[i])
        x = x + gt_f[:, None, :] * y
    return rmsnorm(x, norm_final_g)


ATT_HEADS = 8
ATT_HEAD_DIM = 64
ATT_WIDTH = ATT_HEADS * ATT_HEAD_DIM
IDX_HEADS = 4
IDX_DIM = 64
TOPK_MAX = 256
M_HEADS = 4
M_HEAD_DIM = 128
M_WIDTH = M_HEADS * M_HEAD_DIM
CHUNK = 128
CONV_K = 4
D_FF = 2816
ROPE_THETA = 10000.0
EPS = 1e-6
IN_SIZES = (ATT_WIDTH, ATT_HEAD_DIM, ATT_HEAD_DIM, IDX_HEADS * IDX_DIM, IDX_DIM, IDX_HEADS, 2 * M_WIDTH, M_WIDTH, M_WIDTH, M_HEADS, M_HEADS)
IN_COLS = ATT_WIDTH + 2 * ATT_HEAD_DIM + IDX_HEADS * IDX_DIM + IDX_DIM + IDX_HEADS + 4 * M_WIDTH + 2 * M_HEADS


def rmsnorm_2(x, g):
    xf = x.astype(jnp.float32)
    y = xf * lax.rsqrt(jnp.mean(xf * xf, axis=-1, keepdims=True) + EPS) * g.astype(jnp.float32)
    return y.astype(x.dtype)

def swiglu(x, w_gate, w_up, w_down):
    return (jax.nn.silu(x @ w_gate) * (x @ w_up)) @ w_down

def rope(x, pos):
    half = x.shape[-1] // 2
    inv_freq = ROPE_THETA ** (-jnp.arange(half, dtype=jnp.float32) / half)
    ang = pos.astype(jnp.float32)[:, None] * inv_freq[None, :]
    cos = jnp.cos(ang)[:, None, :]
    sin = jnp.sin(ang)[:, None, :]
    xf = x.astype(jnp.float32)
    x1, x2 = xf[..., :half], xf[..., half:]
    return jnp.concatenate([x1 * cos - x2 * sin, x2 * cos + x1 * sin], axis=-1).astype(x.dtype)

def causal_conv(x, w, b):
    y = lax.conv_general_dilated(x, w.astype(x.dtype), window_strides=(1,), padding=[(CONV_K - 1, 0)],
                                 dimension_numbers=("NWC", "WIO", "NWC"), feature_group_count=x.shape[-1])
    return y + b

def split_columns(proj):
    offsets = np.cumsum(IN_SIZES)[:-1].tolist()
    return jnp.split(proj, offsets, axis=-1)

def dsa_attention(q, k, v, q_idx, k_idx, w_idx):
    B, S = q.shape[0], q.shape[1]
    topk = min(TOPK_MAX, S // 4)
    nb = S // Q_BLOCK
    key_pos = jnp.arange(S, dtype=jnp.int32)

    def to_blocks(a):
        return jnp.moveaxis(a.reshape((B, nb, Q_BLOCK) + a.shape[2:]), 1, 0)

    def gather(src, idx):
        return jax.vmap(lambda sb, ib: sb[ib])(src, idx)

    def one_block(args):
        qb, qib, wb, start = args
        q_pos = start + jnp.arange(Q_BLOCK, dtype=jnp.int32)
        idx_logits = jnp.einsum("bqhd,bsd->bqhs", qib, k_idx, preferred_element_type=jnp.float32) * IDX_DIM ** -0.5
        index_score = jnp.einsum("bqhs,bqh->bqs", jax.nn.relu(idx_logits), wb.astype(jnp.float32))
        index_score = jnp.where(key_pos[None, None, :] <= q_pos[None, :, None], index_score, -jnp.inf)
        _, sel = lax.top_k(index_score, topk)
        k_sel = gather(k, sel)
        v_sel = gather(v, sel)
        logits = jnp.einsum("bqhd,bqkd->bqhk", qb, k_sel, preferred_element_type=jnp.float32) * ATT_HEAD_DIM ** -0.5
        valid = (sel <= q_pos[None, :, None])[:, :, None, :]
        p = jax.nn.softmax(jnp.where(valid, logits, -jnp.inf), axis=-1)
        return jnp.einsum("bqhk,bqkd->bqhd", p.astype(v_sel.dtype), v_sel)

    starts = jnp.arange(nb, dtype=jnp.int32) * Q_BLOCK
    out = lax.map(one_block, (to_blocks(q), to_blocks(q_idx), to_blocks(w_idx), starts))
    return jnp.moveaxis(out, 0, 1).reshape(B, S, ATT_WIDTH)

def mlstm(q, k, v, i_pre, f_pre):
    B, S, NH, d = q.shape
    nc = S // CHUNK

    def chunks(a):
        a = a.astype(jnp.float32).reshape((B, nc, CHUNK, NH) + a.shape[3:])
        return jnp.moveaxis(a, 3, 1)

    qc = chunks(q)
    kc = chunks(k) * d ** -0.5
    vc = chunks(v)
    ic = chunks(i_pre)
    b = jnp.cumsum(jax.nn.log_sigmoid(chunks(f_pre)), axis=-1)
    b_last = b[..., -1]

    a = b_last[..., None] - b + ic
    a_max = a.max(axis=-1)
    wa = jnp.exp(a - a_max[..., None])
    c_chunk = jnp.einsum("bhcl,bhcld,bhcle->bhcde", wa, kc, vc)
    n_chunk = jnp.einsum("bhcl,bhcld->bhcd", wa, kc)

    def step(carry, xs):
        C, n, m = carry
        bl, am, Cc, ncu = xs
        m_new = jnp.maximum(bl + m, am)
        s_old = jnp.exp(bl + m - m_new)
        s_new = jnp.exp(am - m_new)
        C_new = s_old[..., None, None] * C + s_new[..., None, None] * Cc
        n_new = s_old[..., None] * n + s_new[..., None] * ncu
        return (C_new, n_new, m_new), (C, n, m)

    init = (jnp.zeros((B, NH, d, d), jnp.float32), jnp.zeros((B, NH, d), jnp.float32), jnp.zeros((B, NH), jnp.float32))
    xs = (jnp.moveaxis(b_last, 2, 0), jnp.moveaxis(a_max, 2, 0), jnp.moveaxis(c_chunk, 2, 0), jnp.moveaxis(n_chunk, 2, 0))
    _, (C_prev, n_prev, m_prev) = lax.scan(step, init, xs)
    C_prev = jnp.moveaxis(C_prev, 0, 2)
    n_prev = jnp.moveaxis(n_prev, 0, 2)
    m_prev = jnp.moveaxis(m_prev, 0, 2)

    g = b + m_prev[..., None]
    causal = jnp.tril(jnp.ones((CHUNK, CHUNK), dtype=bool))
    dmat = jnp.where(causal, b[..., :, None] - b[..., None, :] + ic[..., None, :], -jnp.inf)
    m_t = jnp.maximum(g, dmat.max(axis=-1))
    w_intra = jnp.exp(dmat - m_t[..., None])
    w_inter = jnp.exp(g - m_t)
    s = jnp.einsum("bhcld,bhcsd->bhcls", qc, kc) * w_intra
    num = w_inter[..., None] * jnp.einsum("bhcld,bhcde->bhcle", qc, C_prev) + jnp.einsum("bhcls,bhcse->bhcle", s, vc)
    den = w_inter * jnp.einsum("bhcld,bhcd->bhcl", qc, n_prev) + s.sum(axis=-1)
    h = num / jnp.maximum(jnp.abs(den), jnp.exp(-m_t))[..., None]
    return jnp.moveaxis(h, 1, 3).reshape(B, S, NH, d)

def hybrid_mixer(h, pos, w_in, conv_w, conv_b, gate_b, q_norm, k_norm, m_norm, w_out):
    B, S, _ = h.shape
    q, k, v, q_idx, k_idx, w_idx, qk_m, v_m, o_m, i_pre, f_pre = split_columns(h @ w_in)
    q = rope(rmsnorm_2(q.reshape(B, S, ATT_HEADS, ATT_HEAD_DIM), q_norm), pos)
    k = rope(rmsnorm_2(k, k_norm)[:, :, None, :], pos)[:, :, 0, :]
    q_idx = rope(q_idx.reshape(B, S, IDX_HEADS, IDX_DIM), pos)
    k_idx = rope(k_idx[:, :, None, :], pos)[:, :, 0, :]
    att = dsa_attention(q, k, v, q_idx, k_idx, w_idx * IDX_HEADS ** -0.5)
    qk_m = jax.nn.silu(causal_conv(qk_m, conv_w, conv_b))
    q_m, k_m = jnp.split(qk_m, 2, axis=-1)
    shape_m = (B, S, M_HEADS, M_HEAD_DIM)
    h_m = mlstm(q_m.reshape(shape_m), k_m.reshape(shape_m), v_m.reshape(shape_m),
                i_pre + gate_b[:M_HEADS], f_pre + gate_b[M_HEADS:])
    h_m = rmsnorm_2(h_m, m_norm).reshape(B, S, M_WIDTH).astype(h.dtype) * jax.nn.sigmoid(o_m)
    return jnp.concatenate([att, h_m], axis=-1) @ w_out

def second_inputs(seed: int = 0) -> dict:
    key = jax.random.key(seed)
    keys = jax.random.split(key, 19)

    def nrm(k, shape, scale):
        return scale * jax.random.normal(k, shape, jnp.float32)

    mix_w = ATT_WIDTH + M_WIDTH
    return {
        "x": nrm(keys[0], (BATCH, SEQ, D_MODEL), 1.0),
        "ffn1_norm": 1.0 + nrm(keys[1], (DEPTH, D_MODEL), 0.02),
        "ffn1_w_gate": nrm(keys[2], (DEPTH, D_MODEL, D_FF), D_MODEL ** -0.5),
        "ffn1_w_up": nrm(keys[3], (DEPTH, D_MODEL, D_FF), D_MODEL ** -0.5),
        "ffn1_w_down": nrm(keys[4], (DEPTH, D_FF, D_MODEL), D_FF ** -0.5),
        "mix_norm": 1.0 + nrm(keys[5], (DEPTH, D_MODEL), 0.02),
        "w_in": nrm(keys[6], (DEPTH, D_MODEL, IN_COLS), D_MODEL ** -0.5),
        "conv_w": nrm(keys[7], (DEPTH, CONV_K, 1, 2 * M_WIDTH), CONV_K ** -0.5),
        "conv_b": nrm(keys[8], (DEPTH, 2 * M_WIDTH), 0.02),
        "gate_b": jnp.concatenate([nrm(keys[9], (DEPTH, M_HEADS), 0.1),
                                   3.0 + nrm(keys[10], (DEPTH, M_HEADS), 0.5)], axis=-1),
        "q_norm": 1.0 + nrm(keys[11], (DEPTH, ATT_HEAD_DIM), 0.02),
        "k_norm": 1.0 + nrm(keys[12], (DEPTH, ATT_HEAD_DIM), 0.02),
        "m_norm": 1.0 + nrm(keys[13], (DEPTH, M_HEADS, M_HEAD_DIM), 0.02),
        "w_out": nrm(keys[14], (DEPTH, mix_w, D_MODEL), mix_w ** -0.5),
        "ffn2_norm": 1.0 + nrm(keys[15], (DEPTH, D_MODEL), 0.02),
        "ffn2_w_gate": nrm(keys[16], (DEPTH, D_MODEL, D_FF), D_MODEL ** -0.5),
        "ffn2_w_up": nrm(keys[17], (DEPTH, D_MODEL, D_FF), D_MODEL ** -0.5),
        "ffn2_w_down": nrm(keys[18], (DEPTH, D_FF, D_MODEL), D_FF ** -0.5),
    }

def second_block(x, ffn1_norm, ffn1_w_gate, ffn1_w_up, ffn1_w_down, mix_norm, w_in, conv_w, conv_b, gate_b,
              q_norm, k_norm, m_norm, w_out, ffn2_norm, ffn2_w_gate, ffn2_w_up, ffn2_w_down):
    pos = jnp.arange(x.shape[1], dtype=jnp.int32)
    for l in range(DEPTH):
        x = x + 0.5 * swiglu(rmsnorm_2(x, ffn1_norm[l]), ffn1_w_gate[l], ffn1_w_up[l], ffn1_w_down[l])
        x = x + hybrid_mixer(rmsnorm_2(x, mix_norm[l]), pos, w_in[l], conv_w[l], conv_b[l], gate_b[l],
                             q_norm[l], k_norm[l], m_norm[l], w_out[l])
        x = x + 0.5 * swiglu(rmsnorm_2(x, ffn2_norm[l]), ffn2_w_gate[l], ffn2_w_up[l], ffn2_w_down[l])
    return x


def setup_inputs(seed=0):
    out = dict(first_inputs(seed))
    for name, value in second_inputs(seed + 1).items():
        if name != "x":
            out[name + "_2"] = value
    return out


def reference(
    x, c, norm_mix_g, norm_ffn_g, ada_w, ada_b, attn_w_in, attn_f_bias, attn_w_o, pool_w,
    pool_scale, router_w, router_bias, exp_w1, exp_w3, exp_w2, norm_final_g, ffn1_norm_2,
    ffn1_w_gate_2, ffn1_w_up_2, ffn1_w_down_2, mix_norm_2, w_in_2, conv_w_2, conv_b_2, gate_b_2,
    q_norm_2, k_norm_2, m_norm_2, w_out_2, ffn2_norm_2, ffn2_w_gate_2, ffn2_w_up_2,
    ffn2_w_down_2,
):
    x = first_block(
        x, c, norm_mix_g, norm_ffn_g, ada_w, ada_b, attn_w_in, attn_f_bias, attn_w_o, pool_w,
        pool_scale, router_w, router_bias, exp_w1, exp_w3, exp_w2, norm_final_g,
    )
    return second_block(
        x, ffn1_norm_2, ffn1_w_gate_2, ffn1_w_up_2, ffn1_w_down_2, mix_norm_2, w_in_2, conv_w_2,
        conv_b_2, gate_b_2, q_norm_2, k_norm_2, m_norm_2, w_out_2, ffn2_norm_2, ffn2_w_gate_2,
        ffn2_w_up_2, ffn2_w_down_2,
    )


_drawn_inputs = setup_inputs


def setup_inputs(seed=0):
    import zlib

    import numpy as np

    out = dict(_drawn_inputs(seed))
    spreads = {}
    factors = {'conv_b_2': 4.303,
     'q_norm_2': 8.0,
     'k_norm_2': 8.0,
     'm_norm_2': 4.308,
     'ffn2_norm_2': 4.339}
    for name, (base, spread) in spreads.items():
        noise = np.random.default_rng([zlib.crc32(name.encode()), seed]).standard_normal(out[name].shape)
        drawn = base * np.exp(spread * noise) if base else spread * noise
        out[name] = jnp.asarray(drawn.astype(out[name].dtype))
    for name, factor in factors.items():
        out[name] = (out[name] * factor).astype(out[name].dtype)
    return out
```

```python
from contextlib import ExitStack

import numpy as np

import concourse.bass as bass
from concourse import mybir

ALU = mybir.AluOpType
ACT = mybir.ActivationFunctionType
F32 = mybir.dt.float32
I32 = mybir.dt.int32
U32 = mybir.dt.uint32
AXX = mybir.AxisListType.X

P = 128
D = 1024
KD = D // P
S = 256
NT = S // P
EPS = 1e-6

HEADS = 16
DH = 64

EXPERTS = 32
GROUPS = 4
PER_GROUP = EXPERTS // GROUPS
DFE = 512
ROWS = 128
NBLK = (2 * S + EXPERTS * (ROWS - 1)) // ROWS
assert NBLK % 2 == 1

DFF = 2816
FCH = 256
NCH = DFF // FCH
FKT = DFF // P

AH = 8
IH = 4
TOPK = min(256, S // 4)
MH = 4
MD = 128
CONVK = 4
C_Q, C_K, C_V, C_QI, C_KI, C_WI, C_QKM, C_VM, C_OM, C_IF = 0, 512, 576, 640, 896, 960, 964, 1988, 2500, 3012
IN_COLS = 3020

SLOT = 4096
RING = 6

NEG = -1e30
GONE = -3e38

CONST = {}
_at = 0
for _name, _n in (("ident", P), ("before", P), ("upto", P), ("ones", P), ("causal", 2 * P), ("cos", NT * 32),
                  ("sin", NT * 32), ("desc32", NT * EXPERTS), ("desc4", NT * GROUPS),
                  ("inv", 4 * 16), ("blk", NBLK), ("neghalf", 1), ("zero", 512)):
    CONST[_name] = (_at, _n)
    _at += _n
NCONST = _at


def constants():
    c = np.zeros((P, NCONST), np.float32)

    def put(name, a):
        at, n = CONST[name]
        c[:, at:at + n] = np.broadcast_to(np.asarray(a, np.float32).reshape(-1, n), (P, n))

    i = np.arange(P)
    put("ident", np.eye(P))
    put("before", i[:, None] < i[None, :])
    put("upto", i[:, None] <= i[None, :])
    put("ones", np.ones((P, P)))
    put("causal", np.concatenate([np.zeros((P, P)), np.where(i[None, :] <= i[:, None], 0.0, NEG)], 1))
    inv_freq = np.float32(10000.0) ** (-np.arange(32, dtype=np.float32) / np.float32(32))
    ang = (np.arange(S, dtype=np.float32)[:, None] * inv_freq[None, :]).astype(np.float32)
    put("cos", np.cos(ang).reshape(NT, P, 32).transpose(1, 0, 2).reshape(P, -1))
    put("sin", np.sin(ang).reshape(NT, P, 32).transpose(1, 0, 2).reshape(P, -1))
    put("desc32", np.tile(np.arange(EXPERTS, 0, -1), NT)[None])
    put("desc4", np.tile(np.arange(GROUPS, 0, -1), NT)[None])
    put("inv", np.stack([1.0 / np.minimum(np.arange(16) + 1, w) for w in (2, 4, 8, 16)]).reshape(1, -1))
    put("blk", np.arange(NBLK)[None])
    put("neghalf", np.full((P, 1), -0.5))
    return c


VEC = {"c": 0, "norm_mix_g": 8, "norm_ffn_g": 24, "ffn1_norm": 40, "mix_norm": 56, "ffn2_norm": 72, "pool_scale": 88,
       "conv_b": 96}
NVEC = 112


class Tally:

    def __init__(self, sems, step=1):
        self.sems, self.count, self.loop = sems, {}, None

    def _value(self, name, n):
        step = 16 if name.startswith(("slot", "xr")) and name.endswith("_full") or name.endswith("_stored") else 1
        if self.loop is None:
            return n * step
        i, per = self.loop
        return i * (per[name] * step) + n * step

    def nth(self, name):
        self.count[name] = self.count.get(name, 0) + 1
        return self.sems[name], self._value(name, self.count[name])

    def peek(self, name):
        return self.sems[name], self._value(name, self.count.get(name, 0) + 1)

    def behind(self, name, n):
        return self.sems[name], self._value(name, self.count[name] - n)

    def skip(self, name):
        self.count[name] = self.count.get(name, 0) + 1

    def enter(self, i, per):
        self.loop, self.start = (i, per), dict(self.count)

    def leave(self, trips):
        per, self.loop = self.loop[1], None
        for name, n in self.count.items():
            d = n - self.start.get(name, 0)
            assert d == per.get(name, 0), f"per trip {name}: {d}, not {per.get(name, 0)}"
            self.count[name] = self.start.get(name, 0) + d * trips


class Sems(dict):
    def __init__(self, make):
        self.make = make

    def __missing__(self, name):
        self[name] = self.make(name)
        return self[name]


def build(nc, A, consts, out, debug=None):
    ctx = ExitStack()
    with ctx:
        def sb(name, shape, dt=F32):
            return ctx.enter_context(nc.sbuf_tensor(name, shape, dt))

        sems = Sems(lambda name: ctx.enter_context(nc.semaphore(name)))

        RINGB = sb("ring", [P, RING, SLOT])
        X = sb("X", [P, NT, D])
        XN = sb("XN", [P, NT, D])
        HT = sb("HT", [P, KD, S])
        GB = sb("GB", [P, D])
        NFG = sb("NFG", [P, D])
        CST = sb("CST", [P, NCONST])
        VR = sb("VR", [P, 3, P])
        VT1 = sb("VT1", [P, NVEC])
        VT2 = sb("VT2", [P, 96])
        VT3 = sb("VT3", [P, 64])
        MOD = sb("MOD", [P, 2, 48])
        CA = sb("CA", [P, KD])
        CT1 = sb("CT1", [P, KD])
        GAIN = sb("GAIN", [P, 2, 2, KD])
        CSG = sb("CSG", [P, KD])
        WR = sb("WR", [P, KD, EXPERTS])
        WF = sb("WF", [P, KD, HEADS])
        WIF = sb("WIF", [P, 2, KD, 8])
        RBIAS = sb("RBIAS", [P, NT, EXPERTS])
        FBIAS = sb("FBIAS", [P, HEADS])
        GATEB = sb("GATEB", [P, 2, 8])
        QN = sb("QN", [P, 2, 64])
        KN = sb("KN", [P, 2, 64])
        MN = sb("MN", [P, 2, 512])
        SS = sb("SS", [P, NT])
        MS = sb("MS", [P, NT])
        RSTD = sb("RSTD", [P, NT])
        SCRATCH = 15900
        SCR = sb("SCR", [P, SCRATCH])
        BLKI = sb("BLKI", [1, NBLK], I32)
        SLOTI = sb("SLOTI", [P, 2 * NT], U32)
        XS = nc.dram_tensor("x_slots", [NBLK * ROWS, D], F32, kind="Internal").ap()
        YS = nc.dram_tensor("y_slots", [NBLK * ROWS, D], F32, kind="Internal").ap()
        x_blocks = XS.rearrange("(b p) n -> b p n", p=ROWS)
        y_blocks = YS.rearrange("(b p) n -> b p n", p=ROWS)
        BK = [ctx.enter_context(nc.psum_tensor(f"bank{b}", [P, 512], F32)) for b in range(8)]

        def cst(name):
            at, n = CONST[name]
            return CST[:, at:at + n]

        ident = cst("ident")
        causal = cst("causal")

        class Carve:
            def __init__(self):
                self.at = 0

            def __call__(self, *dims):
                n = int(np.prod(dims))
                v = SCR[:, self.at:self.at + n]
                self.at += n
                assert self.at <= SCRATCH, self.at
                if len(dims) == 2:
                    v = v.rearrange("p (a b) -> p a b", a=dims[0])
                elif len(dims) == 3:
                    v = v.rearrange("p (a b c) -> p a b c", a=dims[0], b=dims[1])
                return v

        PS = XN[:, :, :].rearrange("p a (b n) -> p a b n", b=2)
        c = Carve()
        QK = c(16, S)
        VV = c(NT, D)
        NF1 = c(HEADS, 256)
        NF0 = c(HEADS, P)
        OT = QK[:, 0:8, :]
        LG = c(2, 384)
        PT = c(2, 384)
        FL, FA, FE, FM = c(NT, HEADS), c(NT, HEADS), c(NT, HEADS), c(NT, HEADS)
        FC = c(NT, HEADS)
        AMX, ASM, ARS = c(2, 2), c(2, 2), c(2, 2)
        c = Carve()
        HP = c(KD, 16 + S)
        W0 = c(KD, 16 + S)
        W1 = c(KD, 16 + S)
        PL = c(KD, S)
        PFIX = c(2, 16)
        YT = c(2, 512)
        c = Carve()
        M_SC, M_SEL, M_M1, M_M2, M_A, M_T = (c(NT, EXPERTS) for _ in range(6))
        M_RK = c(3, EXPERTS)
        M_TOP = c(NT * GROUPS, 8)
        M_GS, M_GC, M_GM, M_GP = c(NT, GROUPS), c(NT, GROUPS), c(NT, GROUPS), c(NT, GROUPS)
        M_R, M_R2, M_RC = c(NT), c(NT), c(NT)
        M_G = c(4, NT)
        M_NB, M_ST = c(EXPERTS), c(EXPERTS)
        M_P0, M_P1 = c(16 + EXPERTS), c(16 + EXPERTS)
        M_BE = c(NBLK, EXPERTS)
        M_BF = c(NBLK)
        XR = c(2, D)
        XB = c(KD, ROWS)
        TH, TA = c(4, ROWS), c(4, ROWS)
        HB = c(4, ROWS)
        YB = c(2, D)
        YR = c(4, D)
        c = Carve()
        F_TH, F_TA, F_H = c(2, 512), c(2, 512), c(2, 2, S)
        c = Carve()
        RO = c(NT, 16, 64)
        MT = RO.rearrange("p t h d -> p (t h d)").rearrange("p (a b) -> p a b", a=8)
        VMA = c(NT, MH, 129)
        OG = c(NT, 512)
        CV = c(KD, 3 + S)
        GI = c(NT, 8)
        VA = c(NT, 64)
        WI = c(NT, IH)
        fork = c.at
        RB = XN[:, :, :].rearrange("p t (h d) -> p t h d", h=16)
        QT = RB.rearrange("p t h d -> p (t h d)").rearrange("p (a b) -> p a b", a=8)
        T1, T2 = c(NT, 640), GB[:, :].rearrange("p (t n) -> p t n", t=NT)
        RSS, RMS, RRS = c(NT * 10), c(NT * 10), c(NT * 10)
        GQ = c(10, 64)
        IR = [c(IH, P), c(IH, 256)]
        IW = c(2, 256)
        M8 = c(8)
        LB = c(256)
        LA = [c(AH, P), c(AH, 256)]
        AM, AS, AR = c(NT, AH), c(NT, AH), c(NT, AH)
        PT0 = HT[:, :, :]
        PT1 = c(AH, P)
        c.at = fork
        CO = c(KD, S)
        TH2 = XN[:, :, :].rearrange("p t (a s) -> p (t a) s", a=4)
        DM = c(8, P)
        ST = c(8, P)
        KW = c(MH, P)
        CS = c(MH, 129)
        IN = c(MH, 129)
        HN = c(8, P)
        HQ = GB[:, :].rearrange("p (m d) -> p m d", m=8)
        LF, LFA, LFE, IMB = c(8), c(8), c(8), c(8)
        BB = c(2, 8)
        MXI, AMAX, M1_ = c(MH), c(MH), c(MH)
        DMX, GG, MTT, BMT = c(8), c(8), c(8), c(8)
        EX, EO = c(24), c(24)
        KWS, WIH, SSUM, DEN, RDEN, HSS, HMS, HRS = (c(8) for _ in range(8))

        loads = [0]
        sem = sems

        x_v = A["x"].rearrange("o (t p) d -> p (o t) d", p=P)
        out_v = out.rearrange("o (t p) d -> p (o t) d", p=P)

        def bfull(b, who):
            return sem[f"bank{b}_full_{who}"]

        def bfree(b):
            return sem[f"bank{b}_free"]

        def bcol(col):
            return col.broadcast_to([P, P])

        def slot(s):
            return RINGB[:, s, :]

        block = ctx.enter_context(nc.Block())
        SMALLS = []

        @block.sync
        def _(sp):
            tally = Tally(sem)
            nth = tally.nth
            ring = [0]

            def load(*parts):
                s = ring[0] % RING
                ring[0] += 1
                sp.wait_ge(*nth(f"slot{s}_free"))
                for src, dst in parts:
                    sp.dma_start(dst(slot(s)), src).then_inc(sem[f"slot{s}_full"], 16)

            def kview(w, c0, n):
                return (w.rearrange("(k p) n -> p k n", p=P)[:, :, c0:c0 + n],
                        lambda v: v[:, 0:KD * n].rearrange("p (k n) -> p k n", k=KD))

            def ada(i):
                for c in range(12):
                    load(kview(A["ada_w"][i], c * 512, 512))

            def experts(i):
                def block(n, par):
                    e = sp.value_load(BLKI[0:1, bass.ds(n, 1)], min_val=0, max_val=EXPERTS - 1)
                    for name in ("exp_w1", "exp_w3"):
                        load((A[name][i][bass.ds(e, 1)].rearrange("e (k p) n -> p (e k) n", p=P),
                              lambda v: v.rearrange("p (k n) -> p k n", k=KD)))
                    load((A["exp_w2"][i][bass.ds(e, 1)].rearrange("e (k p) n -> p (e k) n", p=P),
                          lambda v: v.rearrange("p (k n) -> p k n", k=4)))
                    if par is None:
                        sp.wait_ge(sem["rows_scattered"], 64 * (i + 1))
                    sp.wait_ge(*nth("xr_free"))
                    sp.dma_start(XR[:, par or 0, :], x_blocks[bass.ds(n, 1)].rearrange("e p n -> p (e n)"))\
                        .then_inc(sem[f"xr{par or 0}_full"], 16)

                block(0, None)
                with sp.Fori(0, NBLK // 2) as j:
                    tally.enter(j, {f"slot{s}_free": 1 for s in range(RING)} | {"xr_free": 2})
                    for b in range(2):
                        block(2 * j + (b + 1), (b + 1) % 2)
                    tally.leave(NBLK // 2)

            def ffn(which, l):
                g, u, d = (A[f"{which}_w_{n}"][l] for n in ("gate", "up", "down"))

                def gu(j):
                    load(*((w.rearrange("(k p) n -> p k n", p=P)[:, :, j * FCH:(j + 1) * FCH],
                            lambda v, at=at: v[:, at:at + 2048].rearrange("p (k n) -> p k n", k=KD))
                           for w, at in ((g, 0), (u, 2048))))

                for j in range(0, NCH, 2):
                    gu(j)
                    if j + 1 < NCH:
                        gu(j + 1)
                    n = min(4, FKT - 2 * j)
                    load((d.rearrange("(k p) n -> p k n", p=P)[:, 2 * j:2 * j + n, :],
                          lambda v, n=n: v[:, 0:n * D].rearrange("p (k n) -> p k n", k=n)))

            ada(0)
            w_in = A["attn_w_in"][0]
            for c in range(6):
                load(kview(w_in, c * 512, 512))
            ada(1)
            for c in range(2):
                load(kview(A["attn_w_o"][0], c * 512, 512))
            sp.wait_ge(*nth("routed"))
            experts(0)
            load((A["pool_w"][0].rearrange("g (k p) n -> p (g k) n", p=P),
                  lambda v: v[:, 0:2048].rearrange("p (a n) -> p a n", a=8)))
            sp.wait_ge(*nth("routed"))
            experts(1)
            for l in range(2):
                ffn("ffn1", l)
                w = A["w_in"][l]
                for c0, n in ((C_QKM, 512), (C_QKM + 512, 512), (C_Q, 512), (C_K, C_QKM - C_K), (C_VM, 512), (C_OM, 512)):
                    load(kview(w, c0, n))
                for c in range(2):
                    load(kview(A["w_out"][l], c * 512, 512))
                ffn("ffn2", l)
            sp.wait_ge(*nth("x_final"))
            sp.dma_start(out_v, X[:, :, :]).then_inc(sem["stored"], 16)
            sp.wait_ge(sem["stored"], 16)

        @block.gpsimd
        def _(pool):
            tally = Tally(sem)
            nth = tally.nth
            for b in range(8):
                pool.sem_inc(bfree(b), 1)
            for s in range(RING):
                pool.sem_inc(sem[f"slot{s}_free"], 1)
            pool.sem_inc(sem["xr_free"], 2)
            for q in range(2):
                pool.sem_inc(sem[f"y{q}_stored"], 16)

            def power(dst, src, n, ready):
                pool.wait_ge(*nth("meansq_ready"))
                shape = [P, n]
                nc.gpsimd.tensor_tensor(dst, src, cst("neghalf").broadcast_to(shape), ALU.pow).then_inc(sem[ready], 1)

            def norm():
                power(RSTD[:, :], MS[:, :], NT, "rstd_ready")

            def moe(i):
                norm()
                pool.wait_ge(*nth("slots_ready"))
                if i == 0:
                    pool.wait_ge(sem["zeroed"], 32)
                for q in range(2):
                    for t in range(NT):
                        pool.indirect_dma_start(out=XS, out_offset=bass.IndirectOffsetOnAxis(ap=SLOTI[:, NT * q + t:NT * q + t + 1], axis=0),
                                                in_=XN[:, t, :], in_offset=None).then_inc(sem["rows_scattered"], 16)
                pool.wait_ge(sem["y0_stored"], 16 * (1 + (i + 1) * (NBLK // 2 + 1)))
                pool.wait_ge(sem["y1_stored"], 16 * (1 + (i + 1) * (NBLK // 2)))
                for q in range(2):
                    for t in range(NT):
                        pool.indirect_dma_start(out=YR[:, NT * q + t, :], out_offset=None, in_=YS,
                                                in_offset=bass.IndirectOffsetOnAxis(ap=SLOTI[:, NT * q + t:NT * q + t + 1], axis=0))\
                            .then_inc(sem["rows_gathered"], 16)

            norm()
            moe(0)
            norm()
            moe(1)
            norm()
            for l in range(2):
                norm()
                norm()
                power(RRS[:, :], RMS[:, :], NT * 10, "rstd_ready")
                power(HRS[:, :], HMS[:, :], 8, "rstd_ready")
                norm()

        @block.scalar
        def _(act):
            tally = Tally(sem)
            nth = tally.nth

            def small(dst, src):
                act.dma_start(dst, src).then_inc(sem["smalls"], 16)
                SMALLS.append(1)

            small(CST[:, :], consts)
            small(VR[0:8, 0, :], A["c"].rearrange("o (r p) -> (o r) p", p=P))
            for name, rows in (("norm_mix_g", 16), ("norm_ffn_g", 16), ("ffn1_norm", 16), ("mix_norm", 16),
                               ("ffn2_norm", 16), ("pool_scale", 8), ("conv_b", 16)):
                small(VR[VEC[name]:VEC[name] + rows, 0, :], A[name].rearrange("l (r p) -> (l r) p", p=P))
            small(VR[0:96, 1, :], A["ada_b"].rearrange("l (r p) -> (l r) p", p=P))
            small(VR[0:64, 2, :], A["conv_w"].rearrange("l k o (r p) -> (l k o r) p", p=P))
            small(X[:, :, :], x_v)
            small(WR[:, :, :], A["router_w"].rearrange("(k p) n -> p k n", p=P))
            small(WF[:, :, :], A["attn_w_in"][0].rearrange("(k p) n -> p k n", p=P)[:, :, 3 * D:3 * D + HEADS])
            for l in range(2):
                small(WIF[:, l, :, :], A["w_in"][l].rearrange("(k p) n -> p k n", p=P)[:, :, C_IF:C_IF + 8])
                small(RBIAS[:, l, :], A["router_bias"].rearrange("(o n) -> o n", o=1).broadcast_to([P, EXPERTS]))
                small(GATEB[:, l, :], A["gate_b"][l:l + 1].broadcast_to([P, 8]))
                small(QN[:, l, :], A["q_norm"][l:l + 1].broadcast_to([P, 64]))
                small(KN[:, l, :], A["k_norm"][l:l + 1].broadcast_to([P, 64]))
                small(MN[:, l, :], A["m_norm"][l:l + 1].rearrange("o h d -> o (h d)").broadcast_to([P, 512]))
            small(FBIAS[:, :], A["attn_f_bias"].broadcast_to([P, HEADS]))
            small(NFG[:, :], A["norm_final_g"].rearrange("(o n) -> o n", o=1).broadcast_to([P, D]))

            def step(ins):
                ins.then_inc(sem["act_chain"], 1)
                act.wait_ge(*nth("act_chain"))

            def empty(b, dst, scale=1.0, bias=0.0, src=None, func=ACT.Identity):
                act.wait_ge(*nth(f"bank{b}_full_act"))
                nc.scalar.activation(dst, BK[b][:, :] if src is None else src, func, bias=bias, scale=scale)\
                    .then_inc(bfree(b), 1)

            def squares():
                act.wait_ge(*nth("x_ready"))
                for t in range(NT):
                    ins = nc.scalar.activation(XN[:, t, :], X[:, t, :], ACT.Square, accum_out=SS[:, t:t + 1])
                ins.then_inc(sem["sumsq_ready"], 1)

            def norm(gain, bias, dst=HT, pad=0):
                squares()
                for b in (4, 6):
                    act.wait_ge(*nth(f"bank{b}_full_act"))
                    for j in range(2):
                        k = 2 * (b - 4) + j
                        ins = nc.scalar.activation(dst[:, k, pad:pad + S], BK[b][:, j * S:(j + 1) * S], ACT.Identity,
                                                   scale=gain[:, k:k + 1],
                                                   bias=bias[:, k:k + 1] if bias is not None else 0.0)
                    step(ins)
                    act.sem_inc(bfree(b), 1)
                if pad:
                    act.sem_inc(sem["pool_in_ready"], 1)

            def spread():
                act.wait_ge(*nth("bank4_full_act"))
                step(nc.scalar.activation(GB[:, 0:512], BK[4][:, :], ACT.Identity))
                act.sem_inc(bfree(4), 1)
                act.sem_inc(sem["gate_spread"], 1)

            def moe(i):
                norm(GAIN[:, i, 1, :], MOD[:, i, 24:32])
                for b in (0, 2):
                    empty(b, XN[:, b // 2, 0:512])
                act.wait_ge(*nth("bank4_full_act"))
                step(nc.scalar.activation(M_SC.rearrange("p t e -> p (t e)"), BK[4][:, 0:64], ACT.Exp, scale=-1.0))
                act.sem_inc(bfree(4), 1)
                act.sem_inc(sem["scores_ready"], 1)
                def turned():
                    empty(4, XB[:, 0:4, :].rearrange("p k r -> p (k r)"))

                def block(n, b, last=False):
                    g = 6 if b == 0 else 0
                    act.wait_ge(*nth(f"bank{g}_full_act"))
                    nc.scalar.activation(TH.rearrange("p k r -> p (k r)"), BK[g][:, :], ACT.Tanh, scale=0.5)\
                        .then_inc(sem["tanh_ready"], 1)
                    if not last:
                        turned()
                    act.wait_ge(*nth(f"y{b}_stored"))
                    act.wait_ge(*nth("bank2_full_act"))
                    step(nc.scalar.activation(YB[:, b, 0:512], BK[2][:, :], ACT.Identity))
                    act.sem_inc(bfree(2), 1)
                    act.wait_ge(*nth("y_half"))
                    act.dma_start(y_blocks[bass.ds(n, 1)].rearrange("e p n -> p (e n)"), YB[:, b, :])\
                        .then_inc(sem[f"y{b}_stored"], 16)

                turned()
                with act.Fori(0, NBLK // 2) as j:
                    tally.enter(j, {"bank6_full_act": 1, "bank0_full_act": 1, "bank4_full_act": 2, "bank2_full_act": 2, "act_chain": 2,
                                    "y0_stored": 1, "y1_stored": 1, "y_half": 2})
                    for b in range(2):
                        block(2 * j + b, b)
                    tally.leave(NBLK // 2)
                block(NBLK - 1, 0, last=True)
                spread()

            def ffn(gain):
                norm(gain, None)
                for j in range(NCH):
                    g = 4 + 2 * (j % 2)
                    act.wait_ge(*nth(f"bank{g}_full_act"))
                    nc.scalar.activation(F_TH[:, j % 2, :], BK[g][:, :], ACT.Tanh, scale=0.5)\
                        .then_inc(sem["tanh_ready"], 1)

            act.wait_ge(*nth("vecs_ready"))
            nc.scalar.activation(CT1[:, :], VT1[:, 0:8], ACT.Tanh, scale=0.5).then_inc(sem["tanh_ready"], 1)

            act.wait_ge(*nth("mod_ready"))
            norm(GAIN[:, 0, 0, :], MOD[:, 0, 0:8])
            for h in range(2):
                act.dma_start(XS.rearrange("(b p) n -> p b n", p=ROWS)[:, :, h * 512:(h + 1) * 512],
                              cst("zero").unsqueeze(1).broadcast_to([P, NBLK, 512])).then_inc(sem["zeroed"], 16)
            for n in range(8):
                if n % 2 == 0:
                    empty(n % 4, QK[:, 2 * n:2 * n + 2, :].rearrange("p a s -> p (a s)"), scale=0.125 if n < 4 else 1.0)
            for n in range(4):
                if n % 2 == 0:
                    empty(n, VV[:, n % 2, (n // 2) * 512:(n // 2) * 512 + 512])
            act.wait_ge(*nth("fa_ready"))
            step(nc.scalar.activation(FE.rearrange("p t h -> p (t h)"), FA.rearrange("p t h -> p (t h)"), ACT.Exp, scale=-1.0))
            nc.scalar.activation(FE.rearrange("p t h -> p (t h)"), FE.rearrange("p t h -> p (t h)"), ACT.Ln, bias=1.0)\
                .then_inc(sem["ln_ready"], 1)
            for n in range(4):
                b = n % 4
                act.wait_ge(*nth(f"bank{b}_full_act"))
                nc.scalar.activation(NF1[:, 4 * n:4 * n + 4, 0:P], BK[b][:, :].rearrange("p (h s) -> p h s", h=4),
                                     ACT.Copy, scale=-1.0).then_inc(sem["unmasked_ready"], 1)
            for h in range(HEADS):
                q = h % 2
                act.wait_ge(*nth("logits_ready"))
                nc.scalar.activation(LG[:, q, 0:128], LG[:, q, 0:128], ACT.Exp, bias=AMX[:, q, 0:1],
                                     accum_out=ASM[:, q, 0:1])
                nc.scalar.activation(LG[:, q, 128:384], LG[:, q, 128:384], ACT.Exp, bias=AMX[:, q, 1:2],
                                     accum_out=ASM[:, q, 1:2]).then_inc(sem["exp_ready"], 1)
                if h >= 1:
                    empty(6 + (h - 1) % 2, PT[:, (h - 1) % 2, :], src=BK[6 + (h - 1) % 2][:, 0:384])
            empty(6 + 1, PT[:, 1, :], src=BK[7][:, 0:384])
            spread()
            moe(0)

            act.wait_ge(*nth("mod_ready"))
            norm(GAIN[:, 1, 0, :], MOD[:, 1, 0:8], dst=HP, pad=16)
            spread()
            moe(1)
            squares()

            for l in range(2):
                ffn(VT1[:, VEC["ffn1_norm"] + 8 * l:VEC["ffn1_norm"] + 8 * l + 8])
                norm(VT1[:, VEC["mix_norm"] + 8 * l:VEC["mix_norm"] + 8 * l + 8], None)
                for n in range(4):
                    act.wait_ge(*nth(f"bank{n}_full_act"))
                    nc.scalar.activation(CV[:, 2 * n:2 * n + 2, 3:3 + S],
                                         BK[n][:, :].rearrange("p (a s) -> p a s", a=2), ACT.Identity).then_inc(bfree(n), 1)
                for t in range(NT):
                    act.wait_ge(*nth(f"bank{4 + t}_full_act"))
                    nc.scalar.activation(RB[:, t, 0:8, :], BK[4 + t][:, :].rearrange("p (h d) -> p h d", h=8), ACT.Identity)\
                        .then_inc(bfree(4 + t), 1)
                for t in range(NT):
                    act.wait_ge(*nth(f"bank{6 + t}_full_act"))
                    row = BK[6 + t]
                    for i in range(2):
                        nc.scalar.activation(RB[:, t, 8 + i, :], row[:, 0:64], ACT.Identity)
                        nc.scalar.activation(RB[:, t, 14 + i, :], row[:, 384:448], ACT.Identity)
                    nc.scalar.activation(VA[:, t, :], row[:, 64:128], ACT.Identity)
                    nc.scalar.activation(RB[:, t, 10:14, :], row[:, 128:384].rearrange("p (h d) -> p h d", h=4), ACT.Identity)
                    step(nc.scalar.activation(WI[:, t, :], row[:, 448:452], ACT.Copy, scale=0.5))
                    act.sem_inc(bfree(6 + t), 1)
                act.sem_inc(sem["rows_ready"], 1)
                for t in range(NT):
                    act.wait_ge(*nth(f"bank{t}_full_act"))
                    nc.scalar.activation(VMA[:, t, :, 0:MD], BK[t][:, :].rearrange("p (h d) -> p h d", h=MH), ACT.Identity)\
                        .then_inc(bfree(t), 1)
                for t in range(NT):
                    act.wait_ge(*nth(f"bank{2 + t}_full_act"))
                    nc.scalar.activation(OG[:, t, :], BK[2 + t][:, :], ACT.Tanh, scale=0.5).then_inc(bfree(2 + t), 1)
                for n in (0, 2):
                    empty(n, QT[:, 2 * n:2 * n + 2, :].rearrange("p a s -> p (a s)"))
                act.wait_ge(*nth("bank4_full_act"))
                step(nc.scalar.activation(IR[0].rearrange("p h s -> p (h s)"), BK[4][:, :], ACT.Relu, scale=0.125))
                act.sem_inc(bfree(4), 1)
                act.sem_inc(sem["index_ready"], 1)
                for m in range(2):
                    act.wait_ge(*nth(f"bank{5 + m}_full_act"))
                    step(nc.scalar.activation(IR[1][:, 2 * m:2 * m + 2, :].rearrange("p h s -> p (h s)"), BK[5 + m][:, :],
                                              ACT.Relu, scale=0.125))
                    act.sem_inc(bfree(5 + m), 1)
                act.sem_inc(sem["index_ready"], 1)
                for tb in range(NT):
                    act.wait_ge(*nth("logits_ready"))
                    for h in range(AH):
                        ins = nc.scalar.activation(LA[tb][:, h, :], LA[tb][:, h, :], ACT.Exp, bias=AM[:, tb, h:h + 1],
                                                   accum_out=AS[:, tb, h:h + 1])
                    ins.then_inc(sem["exp_ready"], 1)
                    turned = [(4 + m, PT0[:, 4 * m:4 * m + 4, 0:P]) for m in range(2)] if tb == 0 else \
                        [(6 + m, PT0[:, 4 * m:4 * m + 4, P:2 * P]) for m in range(2)] + \
                        [(4 + m, PT1[:, 4 * m:4 * m + 4, :]) for m in range(2)]
                    for b, dst in turned:
                        act.wait_ge(*nth(f"bank{b}_full_act"))
                        nc.scalar.activation(dst, BK[b][:, :].rearrange("p (h t) -> p h t", h=4), ACT.Identity)\
                            .then_inc(bfree(b), 1)
                for m in range(2):
                    empty(m, MT[:, 2 * m:2 * m + 2, :].rearrange("p a s -> p (a s)"))
                convw = VT3[:, 32 * l:32 * l + 32]
                for k in range(KD):
                    at = VEC["conv_b"] + 8 * l + k
                    ins = nc.scalar.activation(CO[:, k, :], CV[:, k, 0:S], ACT.Identity, scale=convw[:, k:k + 1],
                                               bias=VT1[:, at:at + 1])
                ins.then_inc(sem["tap_ready"], 1)
                act.wait_ge(*nth("fa_ready"))
                step(nc.scalar.activation(LFE[:, :], LFA[:, :], ACT.Exp, scale=-1.0))
                nc.scalar.activation(LFE[:, :], LFE[:, :], ACT.Ln, bias=1.0).then_inc(sem["ln_ready"], 1)
                act.wait_ge(*nth("conv_ready"))
                nc.scalar.activation(TH2[:, :, :], CO[:, :, :], ACT.Tanh, scale=0.5).then_inc(sem["tanh_ready"], 1)
                act.wait_ge(*nth("exponents_ready"))
                nc.scalar.activation(EO[:, :], EX[:, :], ACT.Exp)
                for m in range(8):
                    ins = nc.scalar.activation(DM[:, m, :], DM[:, m, :], ACT.Exp, bias=BMT[:, m:m + 1])
                ins.then_inc(sem["exp_ready"], 1)
                for m in range(2):
                    empty(3 + m, ST[:, 4 * m:4 * m + 4, :].rearrange("p h l -> p (h l)"))
                for m in range(2):
                    empty(5 + m, CS[:, 2 * m:2 * m + 2, :].rearrange("p h e -> p (h e)"), src=BK[5 + m][:, 0:258])
                for m in range(2):
                    empty(3 + m, MT[:, 4 + 2 * m:6 + 2 * m, :].rearrange("p a s -> p (a s)"))
                ffn(VT1[:, VEC["ffn2_norm"] + 8 * l:VEC["ffn2_norm"] + 8 * l + 8])

        @block.vector
        def _(dve):
            tally = Tally(sem)
            nth = tally.nth
            v = nc.vector

            def step(ins):
                ins.then_inc(sem["dve_chain"], 1)
                dve.wait_ge(*nth("dve_chain"))

            def tell(name):
                dve.sem_inc(sem[name], 1)

            def empty(b, dst, src=None):
                dve.wait_ge(*nth(f"bank{b}_full_dve"))
                v.tensor_copy(dst, BK[b][:, :] if src is None else src).then_inc(bfree(b), 1)

            def mean_square():
                dve.wait_ge(*nth("sumsq_ready"))
                v.tensor_scalar(MS[:, :], SS[:, :], 1.0 / D, EPS, ALU.mult, ALU.add).then_inc(sem["meansq_ready"], 1)
                dve.wait_ge(*nth("rstd_ready"))

            def norm(gain, bias, dst=HT, pad=0):
                mean_square()
                for t in range(NT):
                    ins = v.tensor_scalar(XN[:, t, :], X[:, t, :], RSTD[:, t:t + 1], None, ALU.mult)
                ins.then_inc(sem["xn_ready"], 1)
                for b in (5, 7):
                    dve.wait_ge(*nth(f"bank{b}_full_dve"))
                    for j in range(2):
                        k = 2 * (b - 4) + j
                        out, src = dst[:, k, pad:pad + S], BK[b][:, j * S:(j + 1) * S]
                        if bias is None:
                            ins = v.tensor_scalar(out, src, gain[:, k:k + 1], None, ALU.mult)
                        else:
                            ins = v.tensor_scalar(out, src, gain[:, k:k + 1], bias[:, k:k + 1], ALU.mult, ALU.add)
                    step(ins)
                    tell(f"bank{b}_free")

            def add_gated(yt):
                dve.wait_ge(*nth("bank5_full_dve"))
                step(v.tensor_copy(GB[:, 512:1024], BK[5][:, :]))
                tell("bank5_free")
                dve.wait_ge(*nth("gate_spread"))
                for b in range(4):
                    t, h = b // 2, b % 2
                    part = X[:, t, h * 512:(h + 1) * 512]
                    dve.wait_ge(*nth(f"bank{b}_full_dve"))
                    step(v.tensor_tensor(yt[:, b % 2, :], BK[b][:, :], GB[:, h * 512:(h + 1) * 512], ALU.mult))
                    tell(f"bank{b}_free")
                    step(v.tensor_tensor(part, part, yt[:, b % 2, :], ALU.add))
                tell("x_ready")

            def add_plain(factor, last=False):
                for b in range(4):
                    t, h = b // 2, b % 2
                    part = X[:, t, h * 512:(h + 1) * 512]
                    dve.wait_ge(*nth(f"bank{b}_full_dve"))
                    step(v.scalar_tensor_tensor(part, BK[b][:, :], factor, part, ALU.mult, ALU.add))
                    tell(f"bank{b}_free")
                tell("x_final" if last else "x_ready")

            def first_max(dst, src, desc, groups, tmp, mx):
                n = src.shape[2]
                wide = [P, groups, n]
                step(v.tensor_reduce(mx, src, AXX, ALU.max))
                step(v.tensor_tensor(tmp, src, mx.unsqueeze(2).broadcast_to(wide), ALU.is_equal))
                step(v.tensor_tensor(tmp, tmp, desc, ALU.mult))
                step(v.tensor_reduce(mx, tmp, AXX, ALU.max))
                step(v.tensor_tensor(dst, tmp, mx.unsqueeze(2).broadcast_to(wide), ALU.is_equal))

            def route():
                dve.wait_ge(*nth("scores_ready"))
                step(v.tensor_scalar(M_SC, M_SC, 1.0, None, ALU.add))
                step(v.reciprocal(M_SC, M_SC))
                step(v.tensor_tensor(M_SEL, M_SC, RBIAS[:, :, :], ALU.add))
                sel_g = M_SEL.rearrange("p t (g e) -> p (t g) e", g=GROUPS)
                for m in range(NT * GROUPS):
                    ins = v.max(out=M_TOP[:, m, :], in_=sel_g[:, m, :])
                step(ins)
                gs = M_GS.rearrange("p t g -> p (t g)")
                step(v.tensor_tensor(gs, M_TOP[:, :, 0], M_TOP[:, :, 1], ALU.add))
                first_max(M_GM, M_GS, cst("desc4").rearrange("p (t g) -> p t g", t=NT), NT, M_GC, M_R)
                gm, gp = M_GM.rearrange("p t g -> p (t g)"), M_GP.rearrange("p t g -> p (t g)")
                step(v.tensor_scalar(gp, gm, -1.0, -NEG, ALU.add, ALU.mult))
                wide = [P, NT * GROUPS, PER_GROUP]
                step(v.tensor_tensor(sel_g, sel_g, gm.unsqueeze(2).broadcast_to(wide), ALU.mult))
                step(v.tensor_tensor(sel_g, sel_g, gp.unsqueeze(2).broadcast_to(wide), ALU.add))
                desc = cst("desc32").rearrange("p (t e) -> p t e", t=NT)
                first_max(M_M1, M_SEL, desc, NT, M_T, M_R)
                step(v.scalar_tensor_tensor(M_SEL, M_M1, NEG, M_SEL, ALU.mult, ALU.add))
                first_max(M_M2, M_SEL, desc, NT, M_T, M_R)
                step(v.tensor_tensor(M_A, M_M1, M_M2, ALU.add))
                tell("choice_ready")
                for q, m in ((2, M_M1), (3, M_M2)):
                    step(v.tensor_tensor(M_T, m, M_SC, ALU.mult))
                    step(v.tensor_reduce(M_G[:, q, :], M_T, AXX, ALU.add))
                step(v.tensor_tensor(M_RC, M_G[:, 2, :], M_G[:, 3, :], ALU.add))
                step(v.reciprocal(M_RC, M_RC))
                step(v.tensor_tensor(M_G[:, 2:4, :], M_G[:, 2:4, :], M_RC.unsqueeze(1).broadcast_to([P, 2, NT]), ALU.mult))
                dve.wait_ge(*nth("bank5_full_dve"))
                step(v.tensor_copy(M_RK.rearrange("p a e -> p (a e)"), BK[5][:, 0:3 * EXPERTS]))
                tell("bank5_free")
                count = M_RK[:, 2, :]
                step(v.tensor_scalar(M_NB, count, 0.0, None, ALU.is_gt))
                for m in range(1, -(-S // ROWS)):
                    step(v.scalar_tensor_tensor(M_NB, count, float(m * ROWS), M_NB, ALU.is_gt, ALU.add))
                v.memset(M_P0[:, 0:16], 0.0)
                v.memset(M_P1[:, 0:16], 0.0)
                step(v.tensor_copy(M_P0[:, 16:48], M_NB))
                a, b = M_P0, M_P1
                for d in (1, 2, 4, 8, 16):
                    step(v.tensor_tensor(b[:, 16:48], a[:, 16:48], a[:, 16 - d:48 - d], ALU.add))
                    a, b = b, a
                wide = [1, NBLK, EXPERTS]
                step(v.tensor_tensor(M_BE[0:1, :, :], a[0:1, 16:48].unsqueeze(1).broadcast_to(wide),
                                     cst("blk")[0:1, :].unsqueeze(2).broadcast_to(wide), ALU.is_le))
                step(v.tensor_reduce(M_BF[0:1, :], M_BE[0:1, :, :], AXX, ALU.add))
                step(v.tensor_scalar(M_BF[0:1, :], M_BF[0:1, :], float(EXPERTS - 1), None, ALU.min))
                step(v.tensor_copy(BLKI[:, :], M_BF[0:1, :]))
                tell("routed")
                step(v.tensor_tensor(M_ST, a[:, 16:48], M_NB, ALU.subtract))
                step(v.tensor_scalar(M_ST, M_ST, float(ROWS), None, ALU.mult))
                step(v.tensor_tensor(M_RK[:, 0:2, :], M_RK[:, 0:2, :], M_ST.unsqueeze(1).broadcast_to([P, NT, EXPERTS]), ALU.add))
                for q, m in ((0, M_M1), (1, M_M2)):
                    step(v.tensor_tensor(M_T, m, M_RK[:, 0:2, :], ALU.mult))
                    step(v.tensor_reduce(M_G[:, q, :], M_T, AXX, ALU.add))
                step(v.tensor_copy(SLOTI[:, :], M_G[:, 0:2, :].rearrange("p q t -> p (q t)")))
                tell("slots_ready")

            def moe(i):
                first = (32, 138)[i]
                norm(GAIN[:, i, 1, :], MOD[:, i, 24:32])
                for b in (1, 3):
                    empty(b, XN[:, b // 2, 512:1024])
                route()

                def turned():
                    dve.wait_ge(*nth("bank5_full_dve"))
                    tell("xr_free")
                    v.tensor_copy(XB[:, 4:8, :].rearrange("p k r -> p (k r)"), BK[5][:, :]).then_inc(bfree(5), 1)

                def block(b, last=False):
                    g = 6 if b == 0 else 0
                    th, ta, hb = (y.rearrange("p k r -> p (k r)") for y in (TH, TA, HB))
                    dve.wait_ge(*nth("tanh_ready"))
                    step(v.scalar_tensor_tensor(ta, th, 1.0, BK[g][:, :], ALU.add, ALU.mult))
                    tell(f"bank{g}_free")
                    dve.wait_ge(*nth(f"bank{g + 1}_full_dve"))
                    step(v.scalar_tensor_tensor(hb, ta, 0.5, BK[g + 1][:, :], ALU.mult, ALU.mult))
                    tell(f"bank{g + 1}_free")
                    tell("hidden_ready")
                    if not last:
                        turned()
                    dve.wait_ge(*nth(f"y{b}_stored"))
                    dve.wait_ge(*nth("bank3_full_dve"))
                    step(v.tensor_copy(YB[:, b, 512:1024], BK[3][:, :]))
                    tell(f"slot{(first + 3 * b + 2) % RING}_free")
                    tell("bank3_free")
                    tell("y_half")

                turned()
                with dve.Fori(0, NBLK // 2) as j:
                    tally.enter(j, {"dve_chain": 6, "tanh_ready": 2, "bank7_full_dve": 1, "bank1_full_dve": 1, "bank5_full_dve": 2,
                                    "bank3_full_dve": 2, "y0_stored": 1, "y1_stored": 1})
                    for b in range(2):
                        block(b)
                    tally.leave(NBLK // 2)
                block(0, last=True)
                dve.wait_ge(*nth("bank5_full_dve"))
                step(v.tensor_copy(GB[:, 512:1024], BK[5][:, :]))
                tell("bank5_free")
                dve.wait_ge(*nth("gate_spread"))
                dve.wait_ge(sem["rows_gathered"], 64 * (i + 1))
                for t in range(NT):
                    y1, y2 = YR[:, t, :], YR[:, NT + t, :]
                    step(v.tensor_scalar(y1, y1, M_G[:, 2, t:t + 1], None, ALU.mult))
                    step(v.scalar_tensor_tensor(y1, y2, M_G[:, 3, t:t + 1], y1, ALU.mult, ALU.add))
                    step(v.tensor_tensor(y1, y1, GB[:, :], ALU.mult))
                    step(v.tensor_tensor(X[:, t, :], X[:, t, :], y1, ALU.add))
                tell("x_ready")

            def ffn(gain, last=False):
                norm(gain, None)
                for j in range(NCH):
                    q, g = j % 2, 4 + 2 * (j % 2)
                    dve.wait_ge(*nth("tanh_ready"))
                    step(v.scalar_tensor_tensor(F_TA[:, q, :], F_TH[:, q, :], 1.0, BK[g][:, :], ALU.add, ALU.mult))
                    tell(f"bank{g}_free")
                    dve.wait_ge(*nth(f"bank{g + 1}_full_dve"))
                    step(v.scalar_tensor_tensor(F_H[:, q, :, :].rearrange("p a s -> p (a s)"), F_TA[:, q, :], 0.5,
                                                BK[g + 1][:, :], ALU.mult, ALU.mult))
                    tell(f"bank{g + 1}_free")
                    tell("hidden_ready")
                add_plain(0.5, last)

            def log_sigmoid(dst, src, ln):
                dve.wait_ge(*nth("ln_ready"))
                step(v.scalar_tensor_tensor(dst, src, 0.0, ln, ALU.min, ALU.subtract))

            ada_slots = {"ring": 0, "n": 0}

            def ada_slot():
                s, n = ada_slots["ring"] % RING, ada_slots["n"]
                ada_slots["ring"] += 1
                ada_slots["n"] += 1
                w = slot(s).rearrange("p (k n) -> p k n", k=KD)
                dve.wait_ge(*nth(f"slot{s}_full"))
                if n >= 2:
                    dve.wait_ge(*nth("sums_taken"))
                for k in range(KD):
                    acc = PS[:, n % 2, k % 2, :]
                    if k < 2:
                        ins = v.tensor_scalar(acc, w[:, k, :], CA[:, k:k + 1], None, ALU.mult)
                    else:
                        dve.wait_ge(*tally.behind("dve_chain", 1))
                        ins = v.scalar_tensor_tensor(acc, w[:, k, :], CA[:, k:k + 1], acc, ALU.mult, ALU.add)
                    ins.then_inc(sem["dve_chain"], 1)
                    tally.skip("dve_chain")
                dve.wait_ge(*tally.behind("dve_chain", 0))
                tell(f"slot{s}_free")
                tell("sums_ready")

            def modulation(i, b):
                dve.wait_ge(*nth(f"bank{b}_full_dve"))
                step(v.tensor_tensor(MOD[:, i, :], BK[b][:, 0:48], VT2[:, 48 * i:48 * i + 48], ALU.add))
                tell(f"bank{b}_free")
                for w, name in ((0, "norm_mix_g"), (1, "norm_ffn_g")):
                    at = VEC[name] + 8 * i
                    step(v.scalar_tensor_tensor(GAIN[:, i, w, :], MOD[:, i, 8 + 24 * w:16 + 24 * w], 1.0, VT1[:, at:at + 8],
                                                ALU.add, ALU.mult))
                if i == 1:
                    step(v.tensor_tensor(CSG[:, :], MOD[:, 1, 16:24], VT1[:, VEC["pool_scale"]:VEC["pool_scale"] + 8], ALU.mult))
                tell("mod_ready")

            dve.wait_ge(sem["smalls"], 16 * len(SMALLS))
            tell("x_ready")
            empty(0, VT1[:, :], src=BK[0][:, 0:NVEC])
            empty(1, VT2[:, :], src=BK[1][:, 0:96])
            dve.wait_ge(*nth("bank2_full_dve"))
            step(v.tensor_copy(VT3[:, :], BK[2][:, 0:64]))
            tell("bank2_free")
            tell("vecs_ready")
            dve.wait_ge(*nth("tanh_ready"))
            step(v.scalar_tensor_tensor(CA[:, :], CT1[:, :], 1.0, VT1[:, 0:8], ALU.add, ALU.mult))
            step(v.tensor_scalar(CA[:, :], CA[:, :], 0.5, None, ALU.mult))
            tell("c_ready")
            for _ in range(12):
                ada_slot()
            for s_ in range(2):
                dve.wait_ge(*nth("sums_taken"))
            modulation(0, 3)

            norm(GAIN[:, 0, 0, :], MOD[:, 0, 0:8])
            for n in (1, 3, 5, 7):
                dve.wait_ge(*nth(f"bank{n % 4}_full_dve"))
                v.tensor_scalar(QK[:, 2 * n:2 * n + 2, :].rearrange("p a s -> p (a s)"), BK[n % 4][:, :],
                                0.125 if n < 4 else 1.0, None, ALU.mult).then_inc(bfree(n % 4), 1)
            for n in (1, 3):
                empty(n, VV[:, 1, (n // 2) * 512:(n // 2) * 512 + 512])
            FLf, FAf, FEf, FMf, FCf = (y.rearrange("p t h -> p (t h)") for y in (FL, FA, FE, FM, FC))
            dve.wait_ge(*nth("bank4_full_dve"))
            step(v.tensor_tensor(FL, BK[4][:, 0:NT * HEADS].rearrange("p (t h) -> p t h", t=NT),
                                 FBIAS[:, :].unsqueeze(1).broadcast_to([P, NT, HEADS]), ALU.add))
            tell("bank4_free")
            step(v.scalar_tensor_tensor(FAf, FLf, -1.0, FLf, ALU.mult, ALU.max))
            tell("fa_ready")
            log_sigmoid(FMf, FLf, FEf)
            tell("logf_ready")
            dve.wait_ge(*nth("bank5_full_dve"))
            step(v.tensor_copy(FCf, BK[5][:, 0:NT * HEADS]))
            tell("bank5_free")
            tell("f_ready")
            mask = causal[:, P:2 * P].unsqueeze(1).broadcast_to([P, 4, P])
            for n in range(8):
                if n < 4:
                    dve.wait_ge(*nth("unmasked_ready"))
                    dst = NF0[:, 4 * n:4 * n + 4, :]
                else:
                    dve.wait_ge(*nth(f"bank{n}_full_dve"))
                    dst = NF1[:, 4 * (n - 4):4 * (n - 4) + 4, P:2 * P]
                step(v.scalar_tensor_tensor(dst, BK[n][:, :].rearrange("p (h s) -> p h s", h=4), -1.0, mask,
                                            ALU.mult, ALU.add))
                tell(f"bank{n}_free")

            def attend(h):
                q, b = h % 2, 4 + h % 2
                dve.wait_ge(*nth(f"bank{b}_full_dve"))
                v.scalar_tensor_tensor(LG[:, q, 0:128], BK[b][:, 0:128], FC[:, 0, h:h + 1], NF0[:, h, :], ALU.add, ALU.add)
                step(v.scalar_tensor_tensor(LG[:, q, 128:384], BK[b][:, 128:384], FC[:, 1, h:h + 1], NF1[:, h, :],
                                            ALU.add, ALU.add))
                tell(f"bank{b}_free")
                v.tensor_reduce(AMX[:, q, 0:1], LG[:, q, 0:128], AXX, ALU.max, negate=True)
                v.tensor_reduce(AMX[:, q, 1:2], LG[:, q, 128:384], AXX, ALU.max, negate=True).then_inc(sem["logits_ready"], 1)

            def weigh(h):
                q = h % 2
                dve.wait_ge(*nth("exp_ready"))
                step(v.reciprocal(ARS[:, q, :], ASM[:, q, :]))
                v.tensor_scalar(LG[:, q, 0:128], LG[:, q, 0:128], ARS[:, q, 0:1], None, ALU.mult)
                v.tensor_scalar(LG[:, q, 128:384], LG[:, q, 128:384], ARS[:, q, 1:2], None, ALU.mult)\
                    .then_inc(sem["probs_ready"], 1)

            for h in range(HEADS):
                attend(h)
                if h >= 1:
                    weigh(h - 1)
                if h >= 4 and h % 2 == 0:
                    empty(2 + (h // 2) % 2, OT[:, h // 2 - 2, :], src=BK[2 + (h // 2) % 2][:, 0:S])
                if h == 0:
                    for s_ in range(12, 18):
                        tally.skip(f"slot{s_ % RING}_full")
                    ada_slots.update(ring=18, n=0)
                if h < 12:
                    ada_slot()
            for s_ in range(2):
                dve.wait_ge(*nth("sums_taken"))
            modulation(1, 0)
            weigh(HEADS - 1)
            for m in (HEADS // 2 - 2, HEADS // 2 - 1):
                empty(2 + m % 2, OT[:, m, :], src=BK[2 + m % 2][:, 0:S])
            add_gated(YT)
            moe(0)

            for y in (HP, W0, W1):
                v.memset(y[:, :, 0:16], 0.0)
            norm(GAIN[:, 1, 0, :], MOD[:, 1, 0:8], dst=HP, pad=16)
            dve.wait_ge(*nth("pool_in_ready"))
            src, dst = HP, W0
            for g, w in enumerate((2, 4, 8, 16)):
                k = 2 * g
                step(v.tensor_tensor(dst[:, k:8, 16:16 + S], src[:, k:8, 16:16 + S], src[:, k:8, 16 - w // 2:16 + S - w // 2],
                                     ALU.add))
                src, dst = dst, (W1 if dst is W0 else W0)
                ws, h = src[:, k:k + 2, 16:16 + S], HP[:, k:k + 2, 16:16 + S]
                step(v.scalar_tensor_tensor(PL[:, k:k + 2, :], ws, 1.0 / w, h, ALU.mult, ALU.subtract))
                inv = cst("inv")[:, 16 * g:16 * g + 16].unsqueeze(1).broadcast_to([P, 2, 16])
                step(v.tensor_tensor(PFIX, ws[:, :, 0:16], inv, ALU.mult))
                step(v.tensor_tensor(PL[:, k:k + 2, 0:16], PFIX, h[:, :, 0:16], ALU.subtract))
            tell("pooled_ready")
            add_gated(YT)
            moe(1)
            mean_square()
            for t in range(NT):
                ins = v.scalar_tensor_tensor(X[:, t, :], X[:, t, :], RSTD[:, t:t + 1], NFG[:, :], ALU.mult, ALU.mult)
            step(ins)
            tell("x_ready")

            for l in range(2):
                ffn(VT1[:, VEC["ffn1_norm"] + 8 * l:VEC["ffn1_norm"] + 8 * l + 8])
                norm(VT1[:, VEC["mix_norm"] + 8 * l:VEC["mix_norm"] + 8 * l + 8], None)
                v.memset(CV[:, :, 0:3], 0.0)
                v.memset(VMA[:, :, :, MD:MD + 1].rearrange("p t h o -> p t (h o)"), 1.0)
                v.tensor_copy(GQ[:, 0:8, :], QN[:, l, :].unsqueeze(1).broadcast_to([P, 8, 64]))
                v.tensor_copy(GQ[:, 8:10, :], KN[:, l, :].unsqueeze(1).broadcast_to([P, 2, 64]))
                dve.wait_ge(*nth("bank4_full_dve"))
                step(v.tensor_tensor(GI, BK[4][:, 0:16].rearrange("p (t g) -> p t g", t=NT),
                                     GATEB[:, l, :].unsqueeze(1).broadcast_to([P, NT, 8]), ALU.add))
                tell("bank4_free")
                dve.wait_ge(*nth("rows_ready"))
                for t in range(NT):
                    ins = v.tensor_tensor(T1[:, t, :].rearrange("p (h d) -> p h d", h=10), RB[:, t, 0:10, :],
                                          RB[:, t, 0:10, :], ALU.mult)
                step(ins)
                step(v.tensor_reduce(RSS, T1.rearrange("p t (h d) -> p (t h) d", h=10), AXX, ALU.add))
                v.tensor_scalar(RMS, RSS, 1.0 / 64, EPS, ALU.mult, ALU.add).then_inc(sem["meansq_ready"], 1)
                dve.wait_ge(*nth("rstd_ready"))
                for t in range(NT):
                    ins = v.tensor_tensor(RB[:, t, 0:10, :], RB[:, t, 0:10, :],
                                          RRS[:, 10 * t:10 * t + 10].unsqueeze(2).broadcast_to([P, 10, 64]), ALU.mult)
                step(ins)
                for t in range(NT):
                    ins = v.tensor_tensor(RB[:, t, 0:10, :], RB[:, t, 0:10, :], GQ, ALU.mult)
                step(ins)
                for t in range(NT):
                    lo, hi = RB[:, t, :, 0:32], RB[:, t, :, 32:64]
                    cos, sin = (cst(y)[:, 32 * t:32 * t + 32].unsqueeze(1).broadcast_to([P, 16, 32]) for y in ("cos", "sin"))
                    t1, t2 = (y[:, t, 0:512].rearrange("p (h d) -> p h d", h=16) for y in (T1, T2))
                    v.tensor_tensor(t1, lo, cos, ALU.mult)
                    step(v.tensor_tensor(t2, hi, sin, ALU.mult))
                    step(v.tensor_tensor(RO[:, t, :, 0:32], t1, t2, ALU.subtract))
                    v.tensor_tensor(t1, hi, cos, ALU.mult)
                    step(v.tensor_tensor(t2, lo, sin, ALU.mult))
                    step(v.tensor_tensor(RO[:, t, :, 32:64], t1, t2, ALU.add))
                tell("rotated")
                for n in (1, 3):
                    empty(n, QT[:, 2 * n:2 * n + 2, :].rearrange("p a s -> p (a s)"))
                for tb in range(NT):
                    n = P * (tb + 1)
                    mask = causal[:, 2 * P - n:2 * P]
                    lb = LB[:, 0:n]
                    dve.wait_ge(*nth("index_ready"))
                    a, b = IW[:, 0, 0:n], IW[:, 1, 0:n]
                    for j, h in enumerate((0, 2, 1, 3)):
                        step(v.scalar_tensor_tensor(a, IR[tb][:, j, :], WI[:, tb, h:h + 1], mask if j == 0 else a,
                                                    ALU.mult, ALU.add))
                    for _ in range(TOPK // 8):
                        step(v.max(out=M8, in_=a))
                        step(v.match_replace(out=b, in_to_replace=M8, in_values=a, imm_value=GONE))
                        a, b = b, a
                    step(v.tensor_scalar(lb, a, GONE / 2, NEG, ALU.is_gt, ALU.mult))
                    step(v.tensor_tensor(lb, lb, mask, ALU.add))
                    la = LA[tb]
                    banks = (0, 1) if tb == 0 else (2, 3, 0, 1)
                    hh = AH // len(banks)
                    for m, b_ in enumerate(banks):
                        dve.wait_ge(*nth(f"bank{b_}_full_dve"))
                        step(v.scalar_tensor_tensor(la[:, hh * m:hh * m + hh, :],
                                                    BK[b_][:, :].rearrange("p (h s) -> p h s", h=hh), 0.125,
                                                    lb.unsqueeze(1).broadcast_to([P, hh, n]), ALU.mult, ALU.add))
                        tell(f"bank{b_}_free")
                    v.tensor_reduce(AM[:, tb, :], la, AXX, ALU.max, negate=True).then_inc(sem["logits_ready"], 1)
                    dve.wait_ge(*nth("exp_ready"))
                    step(v.reciprocal(AR[:, tb, :], AS[:, tb, :]))
                    v.tensor_tensor(la, la, AR[:, tb, :].unsqueeze(2).broadcast_to([P, AH, n]), ALU.mult)\
                        .then_inc(sem["probs_ready"], 1)
                convw = VT3[:, 32 * l:32 * l + 32]
                dve.wait_ge(*nth("tap_ready"))
                for tap in range(1, CONVK):
                    for k in range(KD):
                        ins = v.scalar_tensor_tensor(CO[:, k, :], CV[:, k, tap:tap + S], convw[:, 8 * tap + k:8 * tap + k + 1],
                                                     CO[:, k, :], ALU.mult, ALU.add)
                    step(ins)
                tell("conv_ready")
                f = GI[:, :, 4:8]
                LF_, LFA_, LFE_, IMB_ = (y.rearrange("p (t h) -> p t h", t=NT) for y in (LF, LFA, LFE, IMB))
                step(v.scalar_tensor_tensor(LFA_, f, -1.0, f, ALU.mult, ALU.max))
                tell("fa_ready")
                log_sigmoid(LF_, f, LFE_)
                tell("logf_ready")
                dve.wait_ge(*nth("tanh_ready"))
                step(v.scalar_tensor_tensor(CO, TH2, 1.0, CO, ALU.add, ALU.mult))
                tell("qk_ready")
                dve.wait_ge(*nth("bank7_full_dve"))
                step(v.tensor_copy(BB.rearrange("p a m -> p (a m)"), BK[7][:, 0:16]))
                tell("bank7_free")
                step(v.tensor_tensor(IMB_, GI[:, :, 0:4], BB[:, 0, :].rearrange("p (t h) -> p t h", t=NT), ALU.subtract))
                tell("imb_ready")
                for ch in range(NT):
                    b = 5 + ch
                    rows = BK[b][:, :].rearrange("p (h s) -> p h s", h=MH)
                    dve.wait_ge(*nth(f"bank{b}_full_dve"))
                    if ch == 0:
                        v.tensor_reduce(MXI, rows, AXX, ALU.max)
                    step(v.tensor_tensor(DM[:, MH * ch:MH * ch + MH, :], rows,
                                         causal[:, P:2 * P].unsqueeze(1).broadcast_to([P, MH, P]), ALU.add))
                    tell(f"bank{b}_free")
                step(v.tensor_reduce(DMX, DM, AXX, ALU.max))
                last = BB[:, 1, 0:MH]
                step(v.tensor_tensor(AMAX, last, MXI, ALU.add))
                step(v.tensor_tensor(M1_, last, AMAX, ALU.max))
                v.tensor_copy(GG[:, 0:MH], BB[:, 0, 0:MH])
                step(v.tensor_tensor(GG[:, MH:8], BB[:, 0, MH:8], M1_, ALU.add))
                step(v.tensor_tensor(MTT, BB[:, 0, :], DMX, ALU.add))
                step(v.tensor_tensor(MTT, MTT, GG, ALU.max))
                v.tensor_tensor(BMT, BB[:, 0, :], MTT, ALU.subtract)
                v.tensor_tensor(EX[:, 0:8], GG, MTT, ALU.subtract)
                v.tensor_scalar(EX[:, 8:16], MTT, -1.0, None, ALU.mult)
                v.tensor_tensor(EX[:, 16:20], IMB[:, 0:MH], MXI, ALU.subtract)
                v.tensor_tensor(EX[:, 20:24], AMAX, M1_, ALU.subtract).then_inc(sem["exponents_ready"], 1)
                dve.wait_ge(*nth("exp_ready"))
                kd = float(MD) ** -0.5
                v.tensor_scalar(WIH[:, 0:MH], EO[:, 4:8], 0.5, None, ALU.mult)
                step(v.scalar_tensor_tensor(KWS[:, 0:MH], EO[:, 16:20], 0.5 * kd, EO[:, 20:24], ALU.mult, ALU.mult))
                for ch in range(NT):
                    dve.wait_ge(*nth(f"bank{ch}_full_dve"))
                    part = DM[:, MH * ch:MH * ch + MH, :]
                    step(v.scalar_tensor_tensor(part, BK[ch][:, :].rearrange("p (h s) -> p h s", h=MH), 0.25 * kd, part,
                                                ALU.mult, ALU.mult))
                    tell(f"bank{ch}_free")
                tell("weighted_ready")
                step(v.tensor_reduce(SSUM, DM, AXX, ALU.add))
                dve.wait_ge(*nth("bank2_full_dve"))
                for h in range(MH):
                    ins = v.tensor_scalar(KW[:, h, :], BK[2][:, P * h:P * h + P], KWS[:, h:h + 1], None, ALU.mult)
                step(ins)
                tell("bank2_free")
                tell("keys_ready")
                for m, b in enumerate((7, 2)):
                    dve.wait_ge(*nth(f"bank{b}_full_dve"))
                    for i in range(2):
                        h = 2 * m + i
                        ins = v.tensor_scalar(IN[:, h, :], BK[b][:, 129 * i:129 * i + 129], WIH[:, h:h + 1], None, ALU.mult)
                    step(ins)
                    tell(f"bank{b}_free")
                v.tensor_copy(DEN[:, 0:MH], SSUM[:, 0:MH])
                step(v.tensor_tensor(DEN[:, MH:8], SSUM[:, MH:8], IN[:, :, MD], ALU.add))
                step(v.scalar_tensor_tensor(DEN, DEN, -1.0, DEN, ALU.mult, ALU.max))
                step(v.tensor_tensor(DEN, DEN, EO[:, 8:16], ALU.max))
                step(v.reciprocal(RDEN, DEN))
                for ch in range(NT):
                    part = HN[:, MH * ch:MH * ch + MH, :]
                    rows = BK[ch][:, :].rearrange("p (h d) -> p h d", h=MH)
                    rden = RDEN[:, MH * ch:MH * ch + MH].unsqueeze(2).broadcast_to([P, MH, MD])
                    dve.wait_ge(*nth(f"bank{ch}_full_dve"))
                    if ch == 0:
                        step(v.tensor_tensor(part, rows, rden, ALU.mult))
                        tell("bank0_free")
                    else:
                        step(v.tensor_tensor(part, rows, IN[:, :, 0:MD], ALU.add))
                        tell("bank1_free")
                        step(v.tensor_tensor(part, part, rden, ALU.mult))
                step(v.tensor_tensor(HQ, HN, HN, ALU.mult))
                step(v.tensor_reduce(HSS, HQ, AXX, ALU.add))
                v.tensor_scalar(HMS, HSS, 1.0 / MD, EPS, ALU.mult, ALU.add).then_inc(sem["meansq_ready"], 1)
                dve.wait_ge(*nth("rstd_ready"))
                step(v.tensor_tensor(HN, HN, HRS.unsqueeze(2).broadcast_to([P, 8, MD]), ALU.mult))
                hn = HN.rearrange("p (c h) d -> p c (h d)", c=NT)
                for ch in range(NT):
                    ins = v.scalar_tensor_tensor(hn[:, ch, :], hn[:, ch, :], 0.5, MN[:, l, :], ALU.mult, ALU.mult)
                step(ins)
                step(v.scalar_tensor_tensor(hn, OG, 1.0, hn, ALU.add, ALU.mult))
                tell("mlstm_ready")
                add_plain(1.0)
                ffn(VT1[:, VEC["ffn2_norm"] + 8 * l:VEC["ffn2_norm"] + 8 * l + 8], last=l == 1)

        @block.tensor
        def _(pe):
            tally = Tally(sem)
            nth, peek = tally.nth, tally.peek
            ring = [0]
            used = []

            def mm(*args, **kw):
                ins = nc.tensor.matmul(*args, **kw)
                if used:
                    ins.then_inc(sem[f"slot{used.pop()}_free"], 1)
                return ins

            def turn(dst, src):
                return mm(dst, src, ident[0:src.shape[0], 0:src.shape[0]], is_transpose=True)

            def fill(b):
                pe.wait_ge(*nth(f"bank{b}_free"))

            def emptied(*banks):
                for b in banks:
                    pe.wait_ge(*peek(f"bank{b}_free"))

            def arrived(parts=1):
                s = ring[0] % RING
                ring[0] += 1
                for _ in range(parts):
                    at = nth(f"slot{s}_full")
                pe.wait_ge(*at)
                return s, slot(s)

            def norm():
                pe.wait_ge(*nth("xn_ready"))
                for b in range(4, 8):
                    fill(b)
                    for j in range(2):
                        k = 2 * (b - 4) + j
                        for t in range(NT):
                            ins = turn(BK[b][:, j * S + t * P:j * S + t * P + P], XN[:, t, k * P:(k + 1) * P])
                    ins.then_inc(bfull(b, "dve" if b % 2 else "act"), 1)

            def spread_gate(col):
                for b in (4, 5):
                    fill(b)
                    for j in range(4):
                        k = 4 * (b - 4) + j
                        ins = mm(BK[b][:, j * P:(j + 1) * P], bcol(col[:, k:k + 1]), ident, start=True, stop=True)
                    ins.then_inc(bfull(b, "dve" if b % 2 else "act"), 1)

            def project(src):
                for h in range(2):
                    s, w = arrived()
                    w = w.rearrange("p (k n) -> p k n", k=KD)
                    for t in range(NT):
                        b = 2 * t + h
                        fill(b)
                        for k in range(KD):
                            ins = mm(BK[b][:, :], src[:, k, t * P:(t + 1) * P], w[:, k, :], start=k == 0, stop=k == KD - 1)
                        ins.then_inc(bfull(b, "dve"), 1)
                    used.append(s)

            def ada_slot(b, c):
                tally.skip(f"slot{ring[0] % RING}_full")
                ring[0] += 1
                pe.wait_ge(*nth("sums_ready"))
                for j in range(4):
                    for i in range(2):
                        ins = mm(BK[b][:, 4 * c + j:4 * c + j + 1], PS[:, c % 2, i, j * P:(j + 1) * P], cst("ones")[:, 0:1],
                                 start=i == 0, stop=i == 1)
                ins.then_inc(sem["sums_taken"], 1)

            def close_ada(b):
                mm(BK[b][:, 48:49], ident, cst("ones")[:, 0:1], start=True, stop=True).then_inc(bfull(b, "dve"), 1)

            def moe():
                norm()
                emptied(4, 5, 6, 7)
                for b in range(4):
                    t, h = b // 2, b % 2
                    fill(b)
                    for j in range(4):
                        ins = turn(BK[b][:, j * P:(j + 1) * P], HT[:, 4 * h + j, t * P:(t + 1) * P])
                    ins.then_inc(bfull(b, "dve" if b % 2 else "act"), 1)
                fill(4)
                for t in range(NT):
                    for k in range(KD):
                        ins = mm(BK[4][:, t * EXPERTS:(t + 1) * EXPERTS], HT[:, k, t * P:(t + 1) * P], WR[:, k, :],
                                 start=k == 0, stop=k == KD - 1)
                ins.then_inc(bfull(4, "act"), 1)
                pe.wait_ge(*nth("choice_ready"))
                fill(5)
                E = EXPERTS
                mm(BK[5][:, 0:E], cst("before"), M_A[:, 0, :], start=True, stop=True)
                mm(BK[5][:, E:2 * E], cst("before"), M_A[:, 1, :], start=True, stop=False)
                mm(BK[5][:, E:2 * E], cst("ones"), M_A[:, 0, :], start=False, stop=True)
                mm(BK[5][:, 2 * E:3 * E], cst("ones"), M_A[:, 0, :], start=True, stop=False)
                mm(BK[5][:, 2 * E:3 * E], cst("ones"), M_A[:, 1, :], start=False, stop=True).then_inc(bfull(5, "dve"), 1)

                def turn_rows(b):
                    pe.wait_ge(*nth(f"xr{b}_full"))
                    for bank in (4, 5):
                        fill(bank)
                        for j in range(4):
                            k = 4 * (bank - 4) + j
                            ins = turn(BK[bank][:, j * ROWS:(j + 1) * ROWS], XR[:, b, k * P:(k + 1) * P])
                        ins.then_inc(bfull(bank, "dve" if bank % 2 else "act"), 1)

                def block(b, last=False):
                    emptied(4, 5)
                    for bank in (6, 7) if b == 0 else (0, 1):
                        fill(bank)
                        s, w = arrived()
                        w = w.rearrange("p (k n) -> p k n", k=KD)
                        for m in range(4):
                            for k in range(KD):
                                ins = mm(BK[bank][:, m * ROWS:(m + 1) * ROWS], w[:, k, m * P:(m + 1) * P], XB[:, k, :],
                                         start=k == 0, stop=k == KD - 1)
                        ins.then_inc(bfull(bank, "dve" if bank % 2 else "act"), 1)
                        used.append(s)
                    if not last:
                        turn_rows((b + 1) % 2)
                    pe.wait_ge(*nth("hidden_ready"))
                    s, w = arrived()
                    w = w.rearrange("p (k n) -> p k n", k=4)
                    for h in range(2):
                        fill(2 + h)
                        for k in range(4):
                            ins = mm(BK[2 + h][:, :], HB[:, k, :], w[:, k, h * 512:(h + 1) * 512], start=k == 0, stop=k == 3)
                        ins.then_inc(bfull(2 + h, "dve" if h else "act"), 1)

                turn_rows(0)
                with pe.Fori(0, NBLK // 2) as j:
                    tally.enter(j, {"hidden_ready": 2, "bank4_free": 2, "bank5_free": 2, "bank6_free": 1, "bank7_free": 1,
                                    "bank0_free": 1, "bank1_free": 1, "bank2_free": 2, "bank3_free": 2, "xr0_full": 1, "xr1_full": 1}
                                | {f"slot{s}_full": 1 for s in range(RING)})
                    for b in range(2):
                        block(b)
                    tally.leave(NBLK // 2)
                block(0, last=True)

            def ffn():
                norm()
                emptied(4, 5, 6, 7)
                down = {}

                def project_down(j):
                    if j % 2 == 0:
                        down[0] = arrived()
                    s, w = down[0]
                    w = w[:, 0:4 * D].rearrange("p (k n) -> p k n", k=4)
                    pe.wait_ge(*nth("hidden_ready"))
                    for b in range(4):
                        t, h = b // 2, b % 2
                        if j == 0:
                            fill(b)
                        for i in range(2):
                            ins = mm(BK[b][:, :], F_H[:, j % 2, i, t * P:(t + 1) * P],
                                     w[:, 2 * (j % 2) + i, h * 512:(h + 1) * 512],
                                     start=j == 0 and i == 0, stop=j == NCH - 1 and i == 1)
                        if j == NCH - 1:
                            ins.then_inc(bfull(b, "dve"), 1)
                    if j % 2 == 1 or j == NCH - 1:
                        used.append(s)

                def project_up(j):
                    g = 4 + 2 * (j % 2)
                    s, w = arrived(2)
                    w = w.rearrange("p (a k n) -> p a k n", a=2, k=KD)
                    for a in range(2):
                        fill(g + a)
                        for m in range(2):
                            for k in range(KD):
                                ins = mm(BK[g + a][:, m * S:(m + 1) * S], w[:, a, k, m * P:(m + 1) * P], HT[:, k, :],
                                         start=k == 0, stop=k == KD - 1)
                        ins.then_inc(bfull(g + a, "dve" if a else "act"), 1)
                    used.append(s)

                for j in range(NCH):
                    project_up(j)
                    if j % 2 == 1:
                        project_down(j - 1)
                        project_down(j)
                project_down(NCH - 1)

            pe.wait_ge(sem["smalls"], 16 * len(SMALLS))
            for b, n in ((0, NVEC), (1, 96), (2, 64)):
                fill(b)
                turn(BK[b][:, 0:n], VR[0:n, b, :]).then_inc(bfull(b, "dve"), 1)
            pe.wait_ge(*nth("c_ready"))
            fill(3)
            for c in range(12):
                ada_slot(3, c)
            close_ada(3)

            norm()
            emptied(4, 5, 6, 7)
            for n in range(8):
                if n % 2 == 0:
                    s, w = arrived()
                    w = w.rearrange("p (k n) -> p k n", k=KD)
                b = n % 4
                fill(b)
                for i in range(2):
                    m = 2 * (n % 2) + i
                    for k in range(KD):
                        ins = mm(BK[b][:, i * S:(i + 1) * S], w[:, k, m * P:(m + 1) * P], HT[:, k, :],
                                 start=k == 0, stop=k == KD - 1)
                ins.then_inc(bfull(b, "dve" if n % 2 else "act"), 1)
                if n % 2 == 1:
                    used.append(s)
            for h in range(2):
                s, w = arrived()
                w = w.rearrange("p (k n) -> p k n", k=KD)
                for t in range(NT):
                    b = 2 * h + t
                    fill(b)
                    for k in range(KD):
                        ins = mm(BK[b][:, :], HT[:, k, t * P:(t + 1) * P], w[:, k, :], start=k == 0, stop=k == KD - 1)
                    ins.then_inc(bfull(b, "dve" if t else "act"), 1)
                used.append(s)
            fill(4)
            for t in range(NT):
                for k in range(KD):
                    ins = mm(BK[4][:, t * HEADS:(t + 1) * HEADS], HT[:, k, t * P:(t + 1) * P], WF[:, k, :],
                             start=k == 0, stop=k == KD - 1)
            ins.then_inc(bfull(4, "dve"), 1)
            pe.wait_ge(*nth("logf_ready"))
            fill(5)
            mm(BK[5][:, 0:HEADS], cst("upto"), FM[:, 0, :], start=True, stop=True)
            mm(BK[5][:, HEADS:2 * HEADS], cst("upto"), FM[:, 1, :], start=True, stop=False)
            mm(BK[5][:, HEADS:2 * HEADS], cst("ones"), FM[:, 0, :], start=False, stop=True).then_inc(bfull(5, "dve"), 1)
            pe.wait_ge(*nth("f_ready"))
            for n in range(8):
                fill(n)
                for j in range(4):
                    h = 4 * (n % 4) + j
                    ins = mm(BK[n][:, j * P:(j + 1) * P], bcol(FC[:, n // 4, h:h + 1]), ident, start=True, stop=True)
                ins.then_inc(bfull(n, "act" if n < 4 else "dve"), 1)

            def scores(h):
                b, at, m = 4 + h % 2, 64 * (h % 2), h // 2
                q, k = QK[at:at + 64, m, :], QK[at:at + 64, 8 + m, :]
                fill(b)
                mm(BK[b][:, 0:P], q[:, 0:P], k[:, 0:P], start=True, stop=True)
                mm(BK[b][:, P:3 * P], q[:, P:2 * P], k[:, :], start=True, stop=True).then_inc(bfull(b, "dve"), 1)

            def turn_probs(h):
                b = 6 + h % 2
                pe.wait_ge(*nth("probs_ready"))
                fill(b)
                for j in range(3):
                    ins = turn(BK[b][:, j * P:(j + 1) * P], LG[:, h % 2, j * P:(j + 1) * P])
                ins.then_inc(bfull(b, "act"), 1)

            def values(h):
                m, at = h // 2, 64 * (h % 2)
                b = 2 + m % 2
                if h % 2 == 0:
                    fill(b)
                emptied(6 + h % 2)
                o, pt = BK[b][at:at + 64, 0:S], PT[:, h % 2, :]
                mm(o, VV[:, 0, h * 64:h * 64 + 64], pt[:, 0:S], start=True, stop=False, skip_group_check=True)
                ins = mm(o[:, P:S], VV[:, 1, h * 64:h * 64 + 64], pt[:, S:S + P], start=False, stop=True,
                         skip_group_check=True)
                if h % 2 == 1:
                    ins.then_inc(bfull(b, "dve"), 1)

            for h in range(HEADS):
                scores(h)
                if h >= 1:
                    turn_probs(h - 1)
                if h >= 2:
                    values(h - 2)
                if h == 1:
                    fill(0)
                if 1 <= h < 13:
                    ada_slot(0, h - 1)
            close_ada(0)
            turn_probs(HEADS - 1)
            values(HEADS - 2)
            values(HEADS - 1)
            spread_gate(MOD[:, 0, 16:24])
            emptied(2, 3)
            project(OT)
            moe()
            spread_gate(MOD[:, 0, 40:48])

            norm()
            pe.wait_ge(*nth("pooled_ready"))
            spread_gate(CSG[:, :])
            s, w = arrived()
            w = w[:, 0:2048].rearrange("p (a n) -> p a n", a=8)
            for b in range(4):
                t, h = b // 2, b % 2
                fill(b)
                for i in range(2):
                    g = 2 * h + i
                    for k in range(2):
                        ins = mm(BK[b][:, i * 256:(i + 1) * 256], PL[:, 2 * g + k, t * P:(t + 1) * P], w[:, 2 * g + k, :],
                                 start=k == 0, stop=k == 1)
                ins.then_inc(bfull(b, "dve"), 1)
            used.append(s)
            moe()
            spread_gate(MOD[:, 1, 40:48])

            for l in range(2):
                ffn()
                norm()
                emptied(4, 5, 6, 7)
                for n in range(4):
                    if n % 2 == 0:
                        s, w = arrived()
                        w = w.rearrange("p (k n) -> p k n", k=KD)
                    fill(n)
                    for i in range(2):
                        m = 2 * (n % 2) + i
                        for k in range(KD):
                            ins = mm(BK[n][:, i * S:(i + 1) * S], w[:, k, m * P:(m + 1) * P], HT[:, k, :],
                                     start=k == 0, stop=k == KD - 1)
                    ins.then_inc(bfull(n, "act"), 1)
                    if n % 2 == 1:
                        used.append(s)
                for b0, cols in ((4, 512), (6, C_QKM - C_K), (0, 512), (2, 512)):
                    s, w = arrived()
                    w = w[:, 0:KD * cols].rearrange("p (k n) -> p k n", k=KD)
                    for t in range(NT):
                        fill(b0 + t)
                        for k in range(KD):
                            ins = mm(BK[b0 + t][:, 0:cols], HT[:, k, t * P:(t + 1) * P], w[:, k, :],
                                     start=k == 0, stop=k == KD - 1)
                        ins.then_inc(bfull(b0 + t, "act"), 1)
                    used.append(s)
                fill(4)
                for t in range(NT):
                    for k in range(KD):
                        ins = mm(BK[4][:, 8 * t:8 * t + 8], HT[:, k, t * P:(t + 1) * P], WIF[:, l, k, :],
                                 start=k == 0, stop=k == KD - 1)
                ins.then_inc(bfull(4, "dve"), 1)
                pe.wait_ge(*nth("rotated"))
                for n in range(4):
                    fill(n)
                    for j in range(2):
                        for t in range(NT):
                            src = RO[:, t, 4 * n + 2 * j:4 * n + 2 * j + 2, :].rearrange("p h d -> p (h d)")
                            ins = turn(BK[n][:, j * S + t * P:j * S + t * P + P], src)
                    ins.then_inc(bfull(n, "dve" if n % 2 else "act"), 1)
                emptied(0, 1, 2, 3)

                def dots(b, q_pairs, k_pair, tb, heads):
                    n = P * (tb + 1)
                    fill(b)
                    for j, h in enumerate(heads):
                        at = 64 * (h % 2)
                        if j and h % 2 != heads[j - 1] % 2:
                            ins.then_inc(sem["pe_chain"], 1)
                            pe.wait_ge(*nth("pe_chain"))
                        ins = mm(BK[b][:, j * n:(j + 1) * n], QT[at:at + 64, q_pairs + h // 2, tb * P:(tb + 1) * P],
                                 QT[at:at + 64, k_pair, 0:n], start=True, stop=True)
                    return ins

                dots(4, 5, 7, 0, (0, 2, 1, 3)).then_inc(bfull(4, "act"), 1)
                dots(5, 5, 7, 1, (0, 2)).then_inc(bfull(5, "act"), 1)
                dots(6, 5, 7, 1, (1, 3)).then_inc(bfull(6, "act"), 1)
                order = (0, 2, 4, 6, 1, 3, 5, 7)
                for m in range(2):
                    dots(m, 0, 4, 0, order[4 * m:4 * m + 4]).then_inc(bfull(m, "dve"), 1)
                for m, b in enumerate((2, 3, 0, 1)):
                    dots(b, 0, 4, 1, order[2 * m:2 * m + 2]).then_inc(bfull(b, "dve"), 1)
                for tb in range(NT):
                    pe.wait_ge(*nth("probs_ready"))
                    for b, h0, kt in (((4, 0, 0), (5, 4, 0)) if tb == 0 else ((6, 0, 0), (7, 4, 0), (4, 0, 1), (5, 4, 1))):
                        fill(b)
                        for j in range(4):
                            ins = turn(BK[b][:, j * P:(j + 1) * P], LA[tb][:, h0 + j, kt * P:(kt + 1) * P])
                        ins.then_inc(bfull(b, "act"), 1)
                emptied(4, 5, 6, 7)
                for m in range(AH // 2):
                    b = m // 2
                    if m % 2 == 0:
                        fill(b)
                    for i in range(2):
                        h = 2 * m + i
                        o = BK[b][64 * i:64 * i + 64, (m % 2) * S:(m % 2) * S + S]
                        h = order.index(h)
                        mm(o, VA[:, 0, :], PT0[:, h, :], start=True, stop=False, skip_group_check=True)
                        ins = mm(o[:, P:S], VA[:, 1, :], PT1[:, h, :], start=False, stop=True, skip_group_check=True)
                    if m % 2 == 1:
                        ins.then_inc(bfull(b, "act"), 1)
                pe.wait_ge(*nth("logf_ready"))
                fill(7)
                mm(BK[7][:, 0:8], cst("upto"), LF, start=True, stop=True)
                mm(BK[7][:, 8:16], cst("ones"), LF, start=True, stop=True).then_inc(bfull(7, "dve"), 1)
                pe.wait_ge(*nth("qk_ready"))
                for ch in range(NT):
                    at = slice(ch * P, (ch + 1) * P)
                    fill(ch)
                    for h in range(MH):
                        ins = mm(BK[ch][:, h * P:(h + 1) * P], CO[:, h, at], CO[:, MH + h, at], start=True, stop=True)
                    ins.then_inc(bfull(ch, "dve"), 1)
                fill(2)
                for h in range(MH):
                    ins = turn(BK[2][:, h * P:(h + 1) * P], CO[:, MH + h, 0:P])
                ins.then_inc(bfull(2, "dve"), 1)
                pe.wait_ge(*nth("imb_ready"))
                for ch in range(NT):
                    fill(5 + ch)
                    for h in range(MH):
                        ins = mm(BK[5 + ch][:, h * P:(h + 1) * P], bcol(IMB[:, MH * ch + h:MH * ch + h + 1]), ident,
                                 start=True, stop=True)
                    ins.then_inc(bfull(5 + ch, "dve"), 1)
                pe.wait_ge(*nth("weighted_ready"))
                for ch in range(NT):
                    fill(3 + ch)
                    for h in range(MH):
                        ins = turn(BK[3 + ch][:, h * P:(h + 1) * P], DM[:, MH * ch + h, :])
                    ins.then_inc(bfull(3 + ch, "act"), 1)
                pe.wait_ge(*nth("keys_ready"))
                for m in range(2):
                    fill(5 + m)
                    for i in range(2):
                        h = 2 * m + i
                        ins = mm(BK[5 + m][:, 129 * i:129 * i + 129], KW[:, h, :], VMA[:, 0, h, :], start=True, stop=True)
                    ins.then_inc(bfull(5 + m, "act"), 1)
                emptied(5, 6)
                for m, b in enumerate((7, 2)):
                    fill(b)
                    for i in range(2):
                        h = 2 * m + i
                        ins = mm(BK[b][:, 129 * i:129 * i + 129], CO[:, h, P:2 * P], CS[:, h, :], start=True, stop=True)
                    ins.then_inc(bfull(b, "dve"), 1)
                emptied(3, 4)
                for ch in range(NT):
                    fill(ch)
                    for h in range(MH):
                        ins = mm(BK[ch][:, h * P:(h + 1) * P], ST[:, MH * ch + h, :], VMA[:, ch, h, 0:MD], start=True, stop=True)
                    ins.then_inc(bfull(ch, "dve"), 1)
                pe.wait_ge(*nth("mlstm_ready"))
                for m in range(2):
                    fill(3 + m)
                    for i in range(2):
                        h = 2 * m + i
                        for ch in range(NT):
                            ins = turn(BK[3 + m][:, i * S + ch * P:i * S + ch * P + P], HN[:, MH * ch + h, :])
                    ins.then_inc(bfull(3 + m, "act"), 1)
                emptied(3, 4)
                project(MT)
                ffn()


_INS = ["x", "c", "norm_mix_g", "norm_ffn_g", "ada_w", "ada_b", "attn_w_in", "attn_f_bias", "attn_w_o", "pool_w",
        "pool_scale", "router_w", "router_bias", "exp_w1", "exp_w3", "exp_w2", "norm_final_g", "ffn1_norm_2",
        "ffn1_w_gate_2", "ffn1_w_up_2", "ffn1_w_down_2", "mix_norm_2", "w_in_2", "conv_w_2", "conv_b_2", "gate_b_2",
        "q_norm_2", "k_norm_2", "m_norm_2", "w_out_2", "ffn2_norm_2", "ffn2_w_gate_2", "ffn2_w_up_2", "ffn2_w_down_2"]


def kernel(**inputs):
    import numpy as _np
    import concourse.bacc as _bacc
    from concourse.bass_utils import run_bass_kernel_spmd as _run

    nc = _bacc.Bacc("TRN2", target_bir_lowering=False, num_devices=1)
    arrays, args = {}, {}

    def given(name, a):
        arrays[f"in_{name}"] = a
        return nc.dram_tensor(f"in_{name}", a.shape, mybir.dt.from_np(a.dtype), kind="ExternalInput").ap()

    for name in _INS:
        args[name.removesuffix("_2")] = given(name, _np.ascontiguousarray(inputs[name]))
    consts = given("constants", constants())
    out = nc.dram_tensor("out_0", (1, S, D), F32, kind="ExternalOutput").ap()
    build(nc, args, consts, out)
    r = _run(nc, [arrays], core_ids=[0])
    return r.results[0]["out_0"]
```

```python
from contextlib import ExitStack

import numpy as np

import concourse.bass as bass
from concourse import mybir

ALU = mybir.AluOpType
ACT = mybir.ActivationFunctionType
F32 = mybir.dt.float32
I32 = mybir.dt.int32
U32 = mybir.dt.uint32
F32R = mybir.dt.float32r
AXX = mybir.AxisListType.X

P = 128
D = 1024
KD = D // P
S = 256
NT = S // P
EPS = 1e-6

HEADS = 16
DH = 64

EXPERTS = 32
GROUPS = 4
PER_GROUP = EXPERTS // GROUPS
DFE = 512
ROWS = 128
NBLK = (2 * S + EXPERTS * (ROWS - 1)) // ROWS
assert NBLK % 2 == 1

DFF = 2816
FCH = 256
NCH = DFF // FCH
FKT = DFF // P
assert NCH % 2 == 1
FFN_STEPS = [(what, j + i) for j in range(0, NCH - 1, 2) for what in ("up", "down") for i in range(2)] + [("down", NCH - 1)]
FFN_STEPS.insert(-2, ("up", NCH - 1))
FFN_SLOTS = NCH + (NCH + 1) // 2
HALF = 2048
SPLITS = 5


def ffn_halves():
    for n, (what, j) in enumerate(FFN_STEPS):
        if what == "up":
            yield j + j // 2, 0, n
            yield j + j // 2, 1, n
        else:
            yield min(3 * (j // 2) + 2, FFN_SLOTS - 1), j % 2, n


FFN_HALVES = list(ffn_halves())
GATE_HALF = [[half[:2] for half in FFN_HALVES].index((j + j // 2, 0)) for j in range(NCH)]

AH = 8
IH = 4
TOPK = min(256, S // 4)
MH = 4
MD = 128
CONVK = 4
C_Q, C_K, C_V, C_QI, C_KI, C_WI, C_QKM, C_VM, C_OM, C_IF = 0, 512, 576, 640, 896, 960, 964, 1988, 2500, 3012
IN_COLS = 3020

SLOT = 4096
RING = 6

NEG = -1e30
GONE = -3e38

ADA_EARLY = 4

CONST = {}
_at = 0
for _name, _n in (("ident", P), ("before", P), ("upto", P), ("ones", P), ("causal", 2 * P), ("cos", NT * 32),
                  ("sin", NT * 32), ("desc32", NT * EXPERTS), ("desc4", NT * GROUPS),
                  ("inv", 4 * 16), ("blk", NBLK), ("neghalf", 1), ("zero", 512)):
    CONST[_name] = (_at, _n)
    _at += _n
NCONST = _at


def constants():
    c = np.zeros((P, NCONST), np.float32)

    def put(name, a):
        at, n = CONST[name]
        c[:, at:at + n] = np.broadcast_to(np.asarray(a, np.float32).reshape(-1, n), (P, n))

    i = np.arange(P)
    put("ident", np.eye(P))
    put("before", i[:, None] < i[None, :])
    put("upto", i[:, None] <= i[None, :])
    put("ones", np.ones((P, P)))
    put("causal", np.concatenate([np.zeros((P, P)), np.where(i[None, :] <= i[:, None], 0.0, NEG)], 1))
    inv_freq = np.float32(10000.0) ** (-np.arange(32, dtype=np.float32) / np.float32(32))
    ang = (np.arange(S, dtype=np.float32)[:, None] * inv_freq[None, :]).astype(np.float32)
    put("cos", np.cos(ang).reshape(NT, P, 32).transpose(1, 0, 2).reshape(P, -1))
    put("sin", np.sin(ang).reshape(NT, P, 32).transpose(1, 0, 2).reshape(P, -1))
    put("desc32", np.tile(np.arange(EXPERTS, 0, -1), NT)[None])
    put("desc4", np.tile(np.arange(GROUPS, 0, -1), NT)[None])
    put("inv", np.stack([1.0 / np.minimum(np.arange(16) + 1, w) for w in (2, 4, 8, 16)]).reshape(1, -1))
    put("blk", np.arange(NBLK)[None])
    put("neghalf", np.full((P, 1), -0.5))
    return c


VEC = {"c": 0, "norm_mix_g": 8, "norm_ffn_g": 24, "ffn1_norm": 40, "mix_norm": 56, "ffn2_norm": 72, "pool_scale": 88,
       "conv_b": 96}
NVEC = 112


class Tally:

    def __init__(self, sems):
        self.sems, self.count, self.loop = sems, {}, None

    def _value(self, name, n):
        step = 16 if name.startswith(("slot", "xr")) and name.endswith("_full") or name.endswith("_stored") else 1
        if self.loop is None:
            return n * step
        i, per = self.loop
        return i * (per[name] * step) + n * step

    def nth(self, name):
        self.count[name] = self.count.get(name, 0) + 1
        return self.sems[name], self._value(name, self.count[name])

    def peek(self, name):
        return self.sems[name], self._value(name, self.count.get(name, 0) + 1)

    def behind(self, name, n):
        return self.sems[name], self._value(name, self.count[name] - n)

    def skip(self, name):
        self.count[name] = self.count.get(name, 0) + 1

    def enter(self, i, per):
        self.loop, self.start = (i, per), dict(self.count)

    def leave(self, trips):
        per, self.loop = self.loop[1], None
        for name, n in self.count.items():
            d = n - self.start.get(name, 0)
            assert d == per.get(name, 0), f"per trip {name}: {d}, not {per.get(name, 0)}"
            self.count[name] = self.start.get(name, 0) + d * trips


class Sems(dict):
    def __init__(self, make):
        self.make = make

    def __missing__(self, name):
        self[name] = self.make(name)
        return self[name]


def build(nc, A, consts, out):
    ctx = ExitStack()
    with ctx:
        def sb(name, shape, dt=F32):
            return ctx.enter_context(nc.sbuf_tensor(name, shape, dt))

        def sb_both(name, shape):
            with nc.sbuf_tensor(name + "_rounded", shape, F32R) as rounded:
                pass
            return sb(name, shape), rounded

        sems = Sems(lambda name: ctx.enter_context(nc.semaphore(name)))

        SLOTS = [sb_both(f"slot{s}", [P, SLOT]) for s in range(RING)]
        X = sb("X", [P, NT, D])
        XN = sb("XN", [P, NT, D])
        HT, HTR = sb_both("HT", [P, KD, S])
        GB = sb("GB", [P, D])
        NFG = sb("NFG", [P, D])
        CST = sb("CST", [P, NCONST])
        VR = sb("VR", [P, 3, P])
        VT1 = sb("VT1", [P, NVEC])
        VT2 = sb("VT2", [P, 96])
        VT3 = sb("VT3", [P, 64])
        MOD = sb("MOD", [P, 2, 48])
        CA = sb("CA", [P, KD])
        CT1 = sb("CT1", [P, KD])
        GAIN = sb("GAIN", [P, 2, 2, KD])
        CSG = sb("CSG", [P, KD])
        WR = sb("WR", [P, KD, EXPERTS])
        WF = sb("WF", [P, KD, HEADS])
        WIF = sb("WIF", [P, 2, KD, 8])
        RBIAS = sb("RBIAS", [P, NT, EXPERTS])
        FBIAS = sb("FBIAS", [P, HEADS])
        GATEB = sb("GATEB", [P, 2, 8])
        QN = sb("QN", [P, 2, 64])
        KN = sb("KN", [P, 2, 64])
        MN = sb("MN", [P, 2, 512])
        SS = sb("SS", [P, NT])
        MS = sb("MS", [P, NT])
        RSTD = sb("RSTD", [P, NT])
        SCRATCH = 15900
        SCR, SCRR = sb_both("SCR", [P, SCRATCH])
        BLKI = sb("BLKI", [1, NBLK], I32)
        SLOTI = sb("SLOTI", [P, 2 * NT], U32)
        XS = nc.dram_tensor("x_slots", [NBLK * ROWS, D], F32, kind="Internal").ap()
        YS = nc.dram_tensor("y_slots", [NBLK * ROWS, D], F32, kind="Internal").ap()
        x_blocks = XS.rearrange("(b p) n -> b p n", p=ROWS)
        y_blocks = YS.rearrange("(b p) n -> b p n", p=ROWS)
        BK = [ctx.enter_context(nc.psum_tensor(f"bank{b}", [P, 512], F32)) for b in range(8)]

        def cst(name):
            at, n = CONST[name]
            return CST[:, at:at + n]

        ident = cst("ident")
        causal = cst("causal")

        class Carve:
            def __init__(self):
                self.at = 0

            def __call__(self, *dims, scratch=None):
                n = int(np.prod(dims))
                v = (SCR if scratch is None else scratch)[:, self.at:self.at + n]
                self.at += n
                assert self.at <= SCRATCH, self.at
                if len(dims) == 2:
                    v = v.rearrange("p (a b) -> p a b", a=dims[0])
                elif len(dims) == 3:
                    v = v.rearrange("p (a b c) -> p a b c", a=dims[0], b=dims[1])
                return v

        PS = XN[:, :, :].rearrange("p a (b n) -> p a b n", b=2)
        c = Carve()
        QK = c(16, S)
        VV = c(NT, D)
        NF1 = c(HEADS, 256)
        NF0 = c(HEADS, P)
        OT = QK[:, 0:8, :]
        LG = c(2, 384)
        PT = c(2, 384)
        FL, FA, FE, FM = c(NT, HEADS), c(NT, HEADS), c(NT, HEADS), c(NT, HEADS)
        FC = c(NT, HEADS)
        AMX, ASM, ARS = c(2, 2), c(2, 2), c(2, 2)
        c = Carve()
        HP = c(KD, 16 + S)
        W0 = c(KD, 16 + S)
        W1 = c(KD, 16 + S)
        PL = c(KD, S)
        PFIX = c(2, 16)
        YT = c(2, 512)
        c = Carve()
        M_SC, M_SEL, M_M1, M_M2, M_A, M_T = (c(NT, EXPERTS) for _ in range(6))
        M_RK = c(3, EXPERTS)
        M_TOP = c(NT * GROUPS, 8)
        M_GS, M_GC, M_GM, M_GP = c(NT, GROUPS), c(NT, GROUPS), c(NT, GROUPS), c(NT, GROUPS)
        M_R, M_R2, M_RC = c(NT), c(NT), c(NT)
        M_G = c(4, NT)
        M_NB, M_ST = c(EXPERTS), c(EXPERTS)
        M_P0, M_P1 = c(16 + EXPERTS), c(16 + EXPERTS)
        M_BE = c(NBLK, EXPERTS)
        M_BF = c(NBLK)
        XR = c(2, D)
        XB = c(KD, ROWS)
        TH, TA = c(4, ROWS), c(4, ROWS)
        HB = c(4, ROWS)
        YB = c(2, D)
        YR = c(4, D)
        c = Carve()
        F_TH, F_TA = c(2, 512), c(512)
        F_HI, F_LO = c(2, 2, S, scratch=SCRR), c(2, 2, S, scratch=SCRR)
        W_HI = c(SPLITS, HALF, scratch=SCRR)
        HT_HI, HT_LO = c(KD, S, scratch=SCRR), HTR[:, :, :]
        c = Carve()
        RO = c(NT, 16, 64)
        MT = RO.rearrange("p t h d -> p (t h d)").rearrange("p (a b) -> p a b", a=8)
        VMA = c(NT, MH, 129)
        OG = c(NT, 512)
        CV = c(KD, 3 + S)
        GI = c(NT, 8)
        VA = c(NT, 64)
        WI = c(NT, IH)
        fork = c.at
        RB = XN[:, :, :].rearrange("p t (h d) -> p t h d", h=16)
        QT = RB.rearrange("p t h d -> p (t h d)").rearrange("p (a b) -> p a b", a=8)
        T1, T2 = c(NT, 640), GB[:, :].rearrange("p (t n) -> p t n", t=NT)
        RSS, RMS, RRS = c(NT * 10), c(NT * 10), c(NT * 10)
        GQ = c(10, 64)
        IR = [c(IH, P), c(IH, 256)]
        IW = c(2, 256)
        M8 = c(8)
        LB = c(256)
        LA = [c(AH, P), c(AH, 256)]
        AM, AS, AR = c(NT, AH), c(NT, AH), c(NT, AH)
        PT0 = HT[:, :, :]
        PT1 = c(AH, P)
        LF, LFA, LFE, IMB = c(8), c(8), c(8), c(8)
        BB = c(2, 8)
        MXI, AMAX, M1_ = c(MH), c(MH), c(MH)
        DMX, GG, MTT, BMT = c(8), c(8), c(8), c(8)
        EX, EO = c(24), c(24)
        KWS, WIH, SSUM, DEN, RDEN, HSS, HMS, HRS = (c(8) for _ in range(8))
        c.at = fork
        CO = c(KD, S)
        TH2 = XN[:, :, :].rearrange("p t (a s) -> p (t a) s", a=4)
        DM = c(8, P)
        ST = c(8, P)
        KW = c(MH, P)
        CS = c(MH, 129)
        IN = c(MH, 129)
        HN = c(8, P)
        HQ = GB[:, :].rearrange("p (m d) -> p m d", m=8)

        loads = [0]
        sem = sems

        x_v = A["x"].rearrange("o (t p) d -> p (o t) d", p=P)
        out_v = out.rearrange("o (t p) d -> p (o t) d", p=P)

        def bfull(b, who):
            return sem[f"bank{b}_full_{who}"]

        def bfree(b):
            return sem[f"bank{b}_free"]

        def bcol(col):
            return col.broadcast_to([P, P])

        def slot(s):
            return SLOTS[s][0][:, :]

        block = ctx.enter_context(nc.Block())
        SMALLS = []
        VECTORS = 11

        @block.sync
        def _(sp):
            tally = Tally(sem)
            nth = tally.nth
            ring = [0]

            def load(*parts):
                s = ring[0] % RING
                ring[0] += 1
                sp.wait_ge(*nth(f"slot{s}_free"))
                for src, dst in parts:
                    sp.dma_start(dst(slot(s)), src).then_inc(sem[f"slot{s}_full"], 16)

            def kview(w, c0, n):
                return (w.rearrange("(k p) n -> p k n", p=P)[:, :, c0:c0 + n],
                        lambda v: v[:, 0:KD * n].rearrange("p (k n) -> p k n", k=KD))

            def ada(*slots):
                for n in slots:
                    load(kview(A["ada_w"][n // 12], n % 12 * 512, 512))

            def experts(i):
                def block(n, par, first=False):
                    e = sp.value_load(BLKI[0:1, bass.ds(n, 1)], min_val=0, max_val=EXPERTS - 1)

                    def hidden(name):
                        load((A[name][i][bass.ds(e, 1)].rearrange("e (k p) n -> p (e k) n", p=P),
                              lambda v: v.rearrange("p (k n) -> p k n", k=KD)))

                    hidden("exp_w1")
                    if first:
                        sp.wait_ge(sem["rows_scattered"], 64 * (i + 1))
                    sp.wait_ge(*nth("xr_free"))
                    sp.dma_start(XR[:, par, :], x_blocks[bass.ds(n, 1)].rearrange("e p n -> p (e n)"))\
                        .then_inc(sem[f"xr{par}_full"], 16)
                    hidden("exp_w3")
                    load((A["exp_w2"][i][bass.ds(e, 1)].rearrange("e (k p) n -> p (e k) n", p=P),
                          lambda v: v.rearrange("p (k n) -> p k n", k=4)))

                block(0, 0, first=True)
                with sp.Fori(0, NBLK // 2) as j:
                    tally.enter(j, {f"slot{s}_free": 1 for s in range(RING)} | {"xr_free": 2})
                    for b in range(2):
                        block(2 * j + (b + 1), (b + 1) % 2)
                    tally.leave(NBLK // 2)

            def ffn(which, l):
                g, u, d = (A[f"{which}_w_{n}"][l] for n in ("gate", "up", "down"))

                def gu(j):
                    load(*((w.rearrange("(k p) n -> p k n", p=P)[:, :, j * FCH:(j + 1) * FCH],
                            lambda v, at=at: v[:, at:at + 2048].rearrange("p (k n) -> p k n", k=KD))
                           for w, at in ((g, 0), (u, 2048))))

                for j in range(0, NCH, 2):
                    gu(j)
                    if j + 1 < NCH:
                        gu(j + 1)
                    n = min(4, FKT - 2 * j)
                    load((d.rearrange("(k p) n -> p k n", p=P)[:, 2 * j:2 * j + n, :],
                          lambda v, n=n: v[:, 0:n * D].rearrange("p (k n) -> p k n", k=n)))

            sp.wait_ge(sem["vectors"], 16 * VECTORS)
            ada(*range(ADA_EARLY))
            w_in = A["attn_w_in"][0]
            for c in range(6):
                load(kview(w_in, c * 512, 512))
                if c < 5:
                    ada(ADA_EARLY + 2 * c, ADA_EARLY + 2 * c + 1)
            ada(*range(ADA_EARLY + 10, 24))
            for c in range(2):
                load(kview(A["attn_w_o"][0], c * 512, 512))
            sp.wait_ge(*nth("routed"))
            experts(0)
            load((A["pool_w"][0].rearrange("g (k p) n -> p (g k) n", p=P),
                  lambda v: v[:, 0:2048].rearrange("p (a n) -> p a n", a=8)))
            sp.wait_ge(*nth("routed"))
            experts(1)
            for l in range(2):
                ffn("ffn1", l)
                w = A["w_in"][l]
                for c0, n in ((C_Q, 512), (C_K, C_QKM - C_K), (C_QKM, 512), (C_QKM + 512, 512), (C_VM, 512), (C_OM, 512)):
                    load(kview(w, c0, n))
                for c in range(2):
                    load(kview(A["w_out"][l], c * 512, 512))
                ffn("ffn2", l)
            sp.wait_ge(*nth("x_final"))
            sp.dma_start(out_v, X[:, :, :]).then_inc(sem["stored"], 16)
            sp.wait_ge(sem["stored"], 16)

        @block.gpsimd
        def _(pool):
            tally = Tally(sem)
            nth = tally.nth
            for b in range(8):
                pool.sem_inc(bfree(b), 1)
            for s in range(RING):
                pool.sem_inc(sem[f"slot{s}_free"], 1)
            pool.sem_inc(sem["xr_free"], 2)
            pool.sem_inc(sem["w_hi_free"], SPLITS)
            for q in range(2):
                pool.sem_inc(sem[f"y{q}_stored"], 16)

            def power(dst, src, n, ready):
                pool.wait_ge(*nth("meansq_ready"))
                shape = [P, n]
                nc.gpsimd.tensor_tensor(dst, src, cst("neghalf").broadcast_to(shape), ALU.pow).then_inc(sem[ready], 1)

            def norm():
                for t in range(NT):
                    power(RSTD[:, t:t + 1], MS[:, t:t + 1], 1, "rstd_ready")

            def moe(i):
                norm()
                pool.wait_ge(*nth("slots_ready"))
                if i == 0:
                    pool.wait_ge(sem["zeroed"], 32)
                for q in range(2):
                    for t in range(NT):
                        pool.indirect_dma_start(out=XS, out_offset=bass.IndirectOffsetOnAxis(ap=SLOTI[:, NT * q + t:NT * q + t + 1], axis=0),
                                                in_=XN[:, t, :], in_offset=None).then_inc(sem["rows_scattered"], 16)
                pool.wait_ge(sem["y0_stored"], 16 * (1 + (i + 1) * (NBLK // 2 + 1)))
                pool.wait_ge(sem["y1_stored"], 16 * (1 + (i + 1) * (NBLK // 2)))
                for t in range(NT):
                    for q in range(2):
                        pool.indirect_dma_start(out=YR[:, NT * q + t, :], out_offset=None, in_=YS,
                                                in_offset=bass.IndirectOffsetOnAxis(ap=SLOTI[:, NT * q + t:NT * q + t + 1], axis=0))\
                            .then_inc(sem[f"rows{t}_gathered"], 16)

            norm()
            moe(0)
            norm()
            moe(1)
            norm()
            for l in range(2):
                norm()
                norm()
                power(RRS[:, :], RMS[:, :], NT * 10, "rstd_ready")
                power(HRS[:, :], HMS[:, :], 8, "rstd_ready")
                norm()

        @block.scalar
        def _(act):
            tally = Tally(sem)
            nth = tally.nth

            def small(dst, src, name="smalls"):
                act.dma_start(dst, src).then_inc(sem[name], 16)
                SMALLS.append(name)

            small(CST[:, :], consts, "vectors")
            small(VR[0:8, 0, :], A["c"].rearrange("o (r p) -> (o r) p", p=P), "vectors")
            for name, rows in (("norm_mix_g", 16), ("norm_ffn_g", 16), ("ffn1_norm", 16), ("mix_norm", 16),
                               ("ffn2_norm", 16), ("pool_scale", 8), ("conv_b", 16)):
                small(VR[VEC[name]:VEC[name] + rows, 0, :], A[name].rearrange("l (r p) -> (l r) p", p=P), "vectors")
            small(VR[0:96, 1, :], A["ada_b"].rearrange("l (r p) -> (l r) p", p=P), "vectors")
            small(VR[0:64, 2, :], A["conv_w"].rearrange("l k o (r p) -> (l k o r) p", p=P), "vectors")
            small(X[:, :, :], x_v)
            small(WR[:, :, :], A["router_w"].rearrange("(k p) n -> p k n", p=P))
            small(WF[:, :, :], A["attn_w_in"][0].rearrange("(k p) n -> p k n", p=P)[:, :, 3 * D:3 * D + HEADS])
            for l in range(2):
                small(WIF[:, l, :, :], A["w_in"][l].rearrange("(k p) n -> p k n", p=P)[:, :, C_IF:C_IF + 8])
                small(RBIAS[:, l, :], A["router_bias"].rearrange("(o n) -> o n", o=1).broadcast_to([P, EXPERTS]))
                small(GATEB[:, l, :], A["gate_b"][l:l + 1].broadcast_to([P, 8]))
                small(QN[:, l, :], A["q_norm"][l:l + 1].broadcast_to([P, 64]))
                small(KN[:, l, :], A["k_norm"][l:l + 1].broadcast_to([P, 64]))
                small(MN[:, l, :], A["m_norm"][l:l + 1].rearrange("o h d -> o (h d)").broadcast_to([P, 512]))
            small(FBIAS[:, :], A["attn_f_bias"].broadcast_to([P, HEADS]))
            small(NFG[:, :], A["norm_final_g"].rearrange("(o n) -> o n", o=1).broadcast_to([P, D]))

            assert SMALLS.count("vectors") == VECTORS

            def step(ins):
                ins.then_inc(sem["act_chain"], 1)
                act.wait_ge(*nth("act_chain"))

            def empty(b, dst, scale=1.0, bias=0.0, src=None, func=ACT.Identity):
                act.wait_ge(*nth(f"bank{b}_full_act"))
                nc.scalar.activation(dst, BK[b][:, :] if src is None else src, func, bias=bias, scale=scale)\
                    .then_inc(bfree(b), 1)

            ring = [0]
            split = {"all": 0, "stage": 0}

            def others(slots):
                for _ in range(slots):
                    tally.skip(f"slot{ring[0] % RING}_full")
                    ring[0] += 1

            def split_to(n):
                while split["stage"] < min(n, len(FFN_HALVES)):
                    at, half, _ = FFN_HALVES[split["stage"]]
                    s = (ring[0] + at) % RING
                    if at > split["slot"]:
                        split["slot"] = at
                        if at % 3 != 2 and at < FFN_SLOTS - 1:
                            tally.skip(f"slot{s}_full")
                        act.wait_ge(*nth(f"slot{s}_full"))
                    act.wait_ge(*nth("w_hi_free"))
                    nc.scalar.activation(W_HI[:, split["all"] % SPLITS, :], slot(s)[:, half * HALF:(half + 1) * HALF],
                                         ACT.Identity).then_inc(sem["w_hi_ready"], 1)
                    split["all"] += 1
                    split["stage"] += 1

            def squares():
                for t in range(NT):
                    act.wait_ge(*nth("x_ready"))
                    nc.scalar.activation(XN[:, t, :], X[:, t, :], ACT.Square, accum_out=SS[:, t:t + 1])\
                        .then_inc(sem["sumsq_ready"], 1)

            def norm(gain, bias, dst=HT, pad=0, ahead=0, split=False):
                split_to(ahead)
                squares()
                for b in (4, 6):
                    act.wait_ge(*nth(f"bank{b}_full_act"))
                    for j in range(2):
                        k = 2 * (b - 4) + j
                        if split:
                            nc.scalar.activation(HT_HI[:, k, :], BK[b][:, j * S:(j + 1) * S], ACT.Identity,
                                                 scale=gain[:, k:k + 1])
                        ins = nc.scalar.activation(dst[:, k, pad:pad + S], BK[b][:, j * S:(j + 1) * S], ACT.Identity,
                                                   scale=gain[:, k:k + 1],
                                                   bias=bias[:, k:k + 1] if bias is not None else 0.0)
                    step(ins)
                    act.sem_inc(bfree(b), 1)
                    if split:
                        act.sem_inc(sem["h_hi_ready"], 1)
                if pad:
                    act.sem_inc(sem["pool_in_ready"], 1)

            def spread():
                act.wait_ge(*nth("bank4_full_act"))
                step(nc.scalar.activation(GB[:, 0:512], BK[4][:, :], ACT.Identity))
                act.sem_inc(bfree(4), 1)
                act.sem_inc(sem["gate_spread"], 1)

            def moe(i):
                norm(GAIN[:, i, 1, :], MOD[:, i, 24:32])
                for b in (0, 2):
                    empty(b, XN[:, b // 2, 0:512])
                act.wait_ge(*nth("bank4_full_act"))
                step(nc.scalar.activation(M_SC.rearrange("p t e -> p (t e)"), BK[4][:, 0:64], ACT.Exp, scale=-1.0))
                act.sem_inc(bfree(4), 1)
                act.sem_inc(sem["scores_ready"], 1)
                def turned():
                    empty(4, XB[:, 0:4, :].rearrange("p k r -> p (k r)"))

                def block(n, b, last=False):
                    g = 6 if b == 0 else 0
                    act.wait_ge(*nth(f"bank{g}_full_act"))
                    nc.scalar.activation(TH.rearrange("p k r -> p (k r)"), BK[g][:, :], ACT.Tanh, scale=0.5)\
                        .then_inc(sem["tanh_ready"], 1)
                    if not last:
                        turned()
                    act.wait_ge(*nth(f"y{b}_stored"))
                    act.wait_ge(*nth("bank2_full_act"))
                    step(nc.scalar.activation(YB[:, b, 0:512], BK[2][:, :], ACT.Identity))
                    act.sem_inc(bfree(2), 1)
                    act.wait_ge(*nth("y_half"))
                    act.dma_start(y_blocks[bass.ds(n, 1)].rearrange("e p n -> p (e n)"), YB[:, b, :])\
                        .then_inc(sem[f"y{b}_stored"], 16)

                turned()
                with act.Fori(0, NBLK // 2) as j:
                    tally.enter(j, {"bank6_full_act": 1, "bank0_full_act": 1, "bank4_full_act": 2, "bank2_full_act": 2, "act_chain": 2,
                                    "y0_stored": 1, "y1_stored": 1, "y_half": 2})
                    for b in range(2):
                        block(2 * j + b, b)
                    tally.leave(NBLK // 2)
                block(NBLK - 1, 0, last=True)
                spread()

            def ffn(gain):
                split["stage"], split["slot"] = 0, -1
                norm(gain, None, ahead=3, split=True)
                for j in range(NCH):
                    g = 4 + 2 * (j % 2)
                    split_to(GATE_HALF[j] + SPLITS)
                    act.wait_ge(*nth(f"bank{g}_full_act"))
                    nc.scalar.activation(F_TH[:, j % 2, :], BK[g][:, :], ACT.Tanh, scale=0.5)\
                        .then_inc(sem["tanh_ready"], 1)
                split_to(len(FFN_HALVES))
                ring[0] += FFN_SLOTS

            act.wait_ge(*nth("vecs_ready"))
            nc.scalar.activation(CT1[:, :], VT1[:, 0:8], ACT.Tanh, scale=0.5).then_inc(sem["tanh_ready"], 1)

            act.wait_ge(*nth("mod_ready"))
            norm(GAIN[:, 0, 0, :], MOD[:, 0, 0:8])
            def clear(h):
                act.dma_start(XS.rearrange("(b p) n -> p b n", p=ROWS)[:, :, h * 512:(h + 1) * 512],
                              cst("zero").unsqueeze(1).broadcast_to([P, NBLK, 512])).then_inc(sem["zeroed"], 16)

            for n in range(8):
                if n % 2 == 0:
                    empty(n % 4, QK[:, 2 * n:2 * n + 2, :].rearrange("p a s -> p (a s)"), scale=0.125 if n < 4 else 1.0)
            for n in range(4):
                if n % 2 == 0:
                    empty(n, VV[:, n % 2, (n // 2) * 512:(n // 2) * 512 + 512])
            act.wait_ge(*nth("fa_ready"))
            step(nc.scalar.activation(FE.rearrange("p t h -> p (t h)"), FA.rearrange("p t h -> p (t h)"), ACT.Exp, scale=-1.0))
            nc.scalar.activation(FE.rearrange("p t h -> p (t h)"), FE.rearrange("p t h -> p (t h)"), ACT.Ln, bias=1.0)\
                .then_inc(sem["ln_ready"], 1)
            for n in range(4):
                b = n % 4
                act.wait_ge(*nth(f"bank{b}_full_act"))
                nc.scalar.activation(NF1[:, 4 * n:4 * n + 4, 0:P], BK[b][:, :].rearrange("p (h s) -> p h s", h=4),
                                     ACT.Copy, scale=-1.0).then_inc(sem["unmasked_ready"], 1)
            for h in range(HEADS):
                if h in (0, 10):
                    clear(h // 10)
                q = h % 2
                act.wait_ge(*nth("logits_ready"))
                nc.scalar.activation(LG[:, q, 0:128], LG[:, q, 0:128], ACT.Exp, bias=AMX[:, q, 0:1],
                                     accum_out=ASM[:, q, 0:1])
                nc.scalar.activation(LG[:, q, 128:384], LG[:, q, 128:384], ACT.Exp, bias=AMX[:, q, 1:2],
                                     accum_out=ASM[:, q, 1:2]).then_inc(sem["exp_ready"], 1)
                if h >= 1:
                    empty(6 + (h - 1) % 2, PT[:, (h - 1) % 2, :], src=BK[6 + (h - 1) % 2][:, 0:384])
            empty(6 + 1, PT[:, 1, :], src=BK[7][:, 0:384])
            spread()
            moe(0)

            act.wait_ge(*nth("mod_ready"))
            norm(GAIN[:, 1, 0, :], MOD[:, 1, 0:8], dst=HP, pad=16)
            spread()
            moe(1)
            squares()

            others(24 + 6 + 2 + 2 * 3 * NBLK + 1)
            for l in range(2):
                ffn(VT1[:, VEC["ffn1_norm"] + 8 * l:VEC["ffn1_norm"] + 8 * l + 8])
                norm(VT1[:, VEC["mix_norm"] + 8 * l:VEC["mix_norm"] + 8 * l + 8], None)
                def before_conv(n, b):
                    act.wait_ge(*nth(f"bank{b}_full_act"))
                    step(nc.scalar.activation(CV[:, 2 * n:2 * n + 2, 3:3 + S],
                                              BK[b][:, :].rearrange("p (a s) -> p a s", a=2), ACT.Identity))
                    act.sem_inc(bfree(b), 1)

                for t in range(NT):
                    act.wait_ge(*nth(f"bank{4 + t}_full_act"))
                    nc.scalar.activation(RB[:, t, 0:8, :], BK[4 + t][:, :].rearrange("p (h d) -> p h d", h=8), ACT.Identity)\
                        .then_inc(bfree(4 + t), 1)
                for t in range(NT):
                    act.wait_ge(*nth(f"bank{6 + t}_full_act"))
                    row = BK[6 + t]
                    for i in range(2):
                        nc.scalar.activation(RB[:, t, 8 + i, :], row[:, 0:64], ACT.Identity)
                        nc.scalar.activation(RB[:, t, 14 + i, :], row[:, 384:448], ACT.Identity)
                    nc.scalar.activation(VA[:, t, :], row[:, 64:128], ACT.Identity)
                    nc.scalar.activation(RB[:, t, 10:14, :], row[:, 128:384].rearrange("p (h d) -> p h d", h=4), ACT.Identity)
                    step(nc.scalar.activation(WI[:, t, :], row[:, 448:452], ACT.Copy, scale=0.5))
                    act.sem_inc(bfree(6 + t), 1)
                act.sem_inc(sem["rows_ready"], 1)
                for n in range(2):
                    before_conv(n, n)
                for n in (0, 2):
                    empty(n, QT[:, 2 * n:2 * n + 2, :].rearrange("p a s -> p (a s)"))
                act.wait_ge(*nth("bank4_full_act"))
                step(nc.scalar.activation(IR[0].rearrange("p h s -> p (h s)"), BK[4][:, :], ACT.Relu, scale=0.125))
                act.sem_inc(bfree(4), 1)
                act.sem_inc(sem["index_ready"], 1)
                for m in range(2):
                    act.wait_ge(*nth(f"bank{5 + m}_full_act"))
                    step(nc.scalar.activation(IR[1][:, 2 * m:2 * m + 2, :].rearrange("p h s -> p (h s)"), BK[5 + m][:, :],
                                              ACT.Relu, scale=0.125))
                    act.sem_inc(bfree(5 + m), 1)
                act.sem_inc(sem["index_ready"], 1)
                for tb in range(NT):
                    act.wait_ge(*nth("logits_ready"))
                    for h in range(AH):
                        ins = nc.scalar.activation(LA[tb][:, h, :], LA[tb][:, h, :], ACT.Exp, bias=AM[:, tb, h:h + 1],
                                                   accum_out=AS[:, tb, h:h + 1])
                    ins.then_inc(sem["exp_ready"], 1)
                    if tb == 0:
                        for n in range(2):
                            before_conv(2 + n, 4 + n)
                convw = VT3[:, 32 * l:32 * l + 32]
                for k in range(KD):
                    at = VEC["conv_b"] + 8 * l + k
                    ins = nc.scalar.activation(CO[:, k, :], CV[:, k, 0:S], ACT.Identity, scale=convw[:, k:k + 1],
                                               bias=VT1[:, at:at + 1])
                ins.then_inc(sem["tap_ready"], 1)
                for t in range(NT):
                    act.wait_ge(*nth(f"bank{6 + t}_full_act"))
                    nc.scalar.activation(VMA[:, t, :, 0:MD], BK[6 + t][:, :].rearrange("p (h d) -> p h d", h=MH), ACT.Identity)\
                        .then_inc(bfree(6 + t), 1)
                act.wait_ge(*nth("fa_ready"))
                step(nc.scalar.activation(LFE[:, :], LFA[:, :], ACT.Exp, scale=-1.0))
                nc.scalar.activation(LFE[:, :], LFE[:, :], ACT.Ln, bias=1.0).then_inc(sem["ln_ready"], 1)
                for t in range(NT):
                    act.wait_ge(*nth(f"bank{4 + t}_full_act"))
                    nc.scalar.activation(OG[:, t, :], BK[4 + t][:, :], ACT.Tanh, scale=0.5).then_inc(bfree(4 + t), 1)
                act.wait_ge(*nth("conv_ready"))
                nc.scalar.activation(TH2[:, :, :], CO[:, :, :], ACT.Tanh, scale=0.5).then_inc(sem["tanh_ready"], 1)
                for b, dst in [(4 + m, PT0[:, 4 * m:4 * m + 4, 0:P]) for m in range(2)] + \
                        [(6 + m, PT0[:, 4 * m:4 * m + 4, P:2 * P]) for m in range(2)] + \
                        [(4 + m, PT1[:, 4 * m:4 * m + 4, :]) for m in range(2)]:
                    act.wait_ge(*nth(f"bank{b}_full_act"))
                    nc.scalar.activation(dst, BK[b][:, :].rearrange("p (h t) -> p h t", h=4), ACT.Identity)\
                        .then_inc(bfree(b), 1)
                for m in range(2):
                    empty(m, MT[:, 2 * m:2 * m + 2, :].rearrange("p a s -> p (a s)"))
                act.wait_ge(*nth("exponents_ready"))
                nc.scalar.activation(EO[:, :], EX[:, :], ACT.Exp)
                for m in range(8):
                    ins = nc.scalar.activation(DM[:, m, :], DM[:, m, :], ACT.Exp, bias=BMT[:, m:m + 1])
                ins.then_inc(sem["exp_ready"], 1)
                for m in range(2):
                    empty(3 + m, ST[:, 4 * m:4 * m + 4, :].rearrange("p h l -> p (h l)"))
                for m in range(2):
                    empty(5 + m, CS[:, 2 * m:2 * m + 2, :].rearrange("p h e -> p (h e)"), src=BK[5 + m][:, 0:258])
                for m in range(2):
                    empty(4 + m, MT[:, 4 + 2 * m:6 + 2 * m, :].rearrange("p a s -> p (a s)"))
                others(6 + 2)
                ffn(VT1[:, VEC["ffn2_norm"] + 8 * l:VEC["ffn2_norm"] + 8 * l + 8])

        @block.vector
        def _(dve):
            tally = Tally(sem)
            nth = tally.nth
            v = nc.vector

            def step(ins):
                ins.then_inc(sem["dve_chain"], 1)
                dve.wait_ge(*nth("dve_chain"))

            def tell(name):
                dve.sem_inc(sem[name], 1)

            def empty(b, dst, src=None):
                dve.wait_ge(*nth(f"bank{b}_full_dve"))
                v.tensor_copy(dst, BK[b][:, :] if src is None else src).then_inc(bfree(b), 1)

            def mean_square():
                for t in range(NT):
                    dve.wait_ge(*nth("sumsq_ready"))
                    v.tensor_scalar(MS[:, t:t + 1], SS[:, t:t + 1], 1.0 / D, EPS, ALU.mult, ALU.add)\
                        .then_inc(sem["meansq_ready"], 1)

            ring = [24 + 6 + 2 + 2 * 3 * NBLK + 1]
            split = {"all": 0, "stage": 0}

            def split_to(n):
                while split["stage"] < min(n, len(FFN_HALVES)):
                    at, half, _ = FFN_HALVES[split["stage"]]
                    s, part = (ring[0] + at) % RING, slice(half * HALF, (half + 1) * HALF)
                    dve.wait_ge(*nth("w_hi_ready"))
                    v.tensor_tensor(SLOTS[s][1][:, part], slot(s)[:, part], W_HI[:, split["all"] % SPLITS, :].bitcast(F32), ALU.subtract)\
                        .then_inc(sem["w_lo_ready"], 1)
                    split["all"] += 1
                    split["stage"] += 1

            def norm(gain, bias, dst=HT, pad=0, ahead=0, split=False):
                mean_square()
                for t in range(NT):
                    dve.wait_ge(*nth("rstd_ready"))
                    v.tensor_scalar(XN[:, t, :], X[:, t, :], RSTD[:, t:t + 1], None, ALU.mult).then_inc(sem["xn_ready"], 1)
                split_to(ahead)
                for b in (5, 7):
                    dve.wait_ge(*nth(f"bank{b}_full_dve"))
                    for j in range(2):
                        k = 2 * (b - 4) + j
                        out, src = dst[:, k, pad:pad + S], BK[b][:, j * S:(j + 1) * S]
                        if split:
                            v.tensor_scalar(HT_HI[:, k, :], src, gain[:, k:k + 1], None, ALU.mult)
                        if bias is None:
                            ins = v.tensor_scalar(out, src, gain[:, k:k + 1], None, ALU.mult)
                        else:
                            ins = v.tensor_scalar(out, src, gain[:, k:k + 1], bias[:, k:k + 1], ALU.mult, ALU.add)
                    step(ins)
                    tell(f"bank{b}_free")
                    if split:
                        half = slice(2 * (b - 5), 2 * (b - 5) + 4)
                        dve.wait_ge(*nth("h_hi_ready"))
                        v.tensor_tensor(HT_LO[:, half, :], HT[:, half, :], HT_HI[:, half, :].bitcast(F32), ALU.subtract)\
                            .then_inc(sem["h_lo_ready"], 1)

            def add_gated(yt):
                dve.wait_ge(*nth("bank5_full_dve"))
                step(v.tensor_copy(GB[:, 512:1024], BK[5][:, :]))
                tell("bank5_free")
                dve.wait_ge(*nth("gate_spread"))
                for b in range(4):
                    t, h = b // 2, b % 2
                    part = X[:, t, h * 512:(h + 1) * 512]
                    dve.wait_ge(*nth(f"bank{b}_full_dve"))
                    step(v.tensor_tensor(yt[:, b % 2, :], BK[b][:, :], GB[:, h * 512:(h + 1) * 512], ALU.mult))
                    tell(f"bank{b}_free")
                    step(v.tensor_tensor(part, part, yt[:, b % 2, :], ALU.add))
                    if h == 1:
                        tell("x_ready")

            def add_plain(factor, last=False):
                for b in range(4):
                    t, h = b // 2, b % 2
                    part = X[:, t, h * 512:(h + 1) * 512]
                    dve.wait_ge(*nth(f"bank{b}_full_dve"))
                    step(v.scalar_tensor_tensor(part, BK[b][:, :], factor, part, ALU.mult, ALU.add))
                    tell(f"bank{b}_free")
                    if h == 1 and not last:
                        tell("x_ready")
                if last:
                    tell("x_final")

            def first_max(dst, src, desc, groups, tmp, mx):
                n = src.shape[2]
                wide = [P, groups, n]
                step(v.tensor_reduce(mx, src, AXX, ALU.max))
                step(v.tensor_tensor(tmp, src, mx.unsqueeze(2).broadcast_to(wide), ALU.is_equal))
                step(v.tensor_tensor(tmp, tmp, desc, ALU.mult))
                step(v.tensor_reduce(mx, tmp, AXX, ALU.max))
                step(v.tensor_tensor(dst, tmp, mx.unsqueeze(2).broadcast_to(wide), ALU.is_equal))

            def route():
                dve.wait_ge(*nth("scores_ready"))
                step(v.tensor_scalar(M_SC, M_SC, 1.0, None, ALU.add))
                step(v.reciprocal(M_SC, M_SC))
                step(v.tensor_tensor(M_SEL, M_SC, RBIAS[:, :, :], ALU.add))
                sel_g = M_SEL.rearrange("p t (g e) -> p (t g) e", g=GROUPS)
                for m in range(NT * GROUPS):
                    ins = v.max(out=M_TOP[:, m, :], in_=sel_g[:, m, :])
                step(ins)
                gs = M_GS.rearrange("p t g -> p (t g)")
                step(v.tensor_tensor(gs, M_TOP[:, :, 0], M_TOP[:, :, 1], ALU.add))
                first_max(M_GM, M_GS, cst("desc4").rearrange("p (t g) -> p t g", t=NT), NT, M_GC, M_R)
                gm, gp = M_GM.rearrange("p t g -> p (t g)"), M_GP.rearrange("p t g -> p (t g)")
                step(v.tensor_scalar(gp, gm, -1.0, -NEG, ALU.add, ALU.mult))
                wide = [P, NT * GROUPS, PER_GROUP]
                step(v.tensor_tensor(sel_g, sel_g, gm.unsqueeze(2).broadcast_to(wide), ALU.mult))
                step(v.tensor_tensor(sel_g, sel_g, gp.unsqueeze(2).broadcast_to(wide), ALU.add))
                desc = cst("desc32").rearrange("p (t e) -> p t e", t=NT)
                first_max(M_M1, M_SEL, desc, NT, M_T, M_R)
                step(v.scalar_tensor_tensor(M_SEL, M_M1, NEG, M_SEL, ALU.mult, ALU.add))
                first_max(M_M2, M_SEL, desc, NT, M_T, M_R)
                step(v.tensor_tensor(M_A, M_M1, M_M2, ALU.add))
                tell("choice_ready")
                for q, m in ((2, M_M1), (3, M_M2)):
                    step(v.tensor_tensor(M_T, m, M_SC, ALU.mult))
                    step(v.tensor_reduce(M_G[:, q, :], M_T, AXX, ALU.add))
                step(v.tensor_tensor(M_RC, M_G[:, 2, :], M_G[:, 3, :], ALU.add))
                step(v.reciprocal(M_RC, M_RC))
                step(v.tensor_tensor(M_G[:, 2:4, :], M_G[:, 2:4, :], M_RC.unsqueeze(1).broadcast_to([P, 2, NT]), ALU.mult))
                dve.wait_ge(*nth("bank5_full_dve"))
                step(v.tensor_copy(M_RK.rearrange("p a e -> p (a e)"), BK[5][:, 0:3 * EXPERTS]))
                tell("bank5_free")
                count = M_RK[:, 2, :]
                step(v.tensor_scalar(M_NB, count, 0.0, None, ALU.is_gt))
                for m in range(1, -(-S // ROWS)):
                    step(v.scalar_tensor_tensor(M_NB, count, float(m * ROWS), M_NB, ALU.is_gt, ALU.add))
                v.memset(M_P0[:, 0:16], 0.0)
                v.memset(M_P1[:, 0:16], 0.0)
                step(v.tensor_copy(M_P0[:, 16:48], M_NB))
                a, b = M_P0, M_P1
                for d in (1, 2, 4, 8, 16):
                    step(v.tensor_tensor(b[:, 16:48], a[:, 16:48], a[:, 16 - d:48 - d], ALU.add))
                    a, b = b, a
                step(v.tensor_tensor(M_ST, a[:, 16:48], M_NB, ALU.subtract))
                step(v.tensor_scalar(M_ST, M_ST, float(ROWS), None, ALU.mult))
                step(v.tensor_tensor(M_RK[:, 0:2, :], M_RK[:, 0:2, :], M_ST.unsqueeze(1).broadcast_to([P, NT, EXPERTS]), ALU.add))
                for q, m in ((0, M_M1), (1, M_M2)):
                    step(v.tensor_tensor(M_T, m, M_RK[:, 0:2, :], ALU.mult))
                    step(v.tensor_reduce(M_G[:, q, :], M_T, AXX, ALU.add))
                step(v.tensor_copy(SLOTI[:, :], M_G[:, 0:2, :].rearrange("p q t -> p (q t)")))
                tell("slots_ready")
                wide = [1, NBLK, EXPERTS]
                step(v.tensor_tensor(M_BE[0:1, :, :], a[0:1, 16:48].unsqueeze(1).broadcast_to(wide),
                                     cst("blk")[0:1, :].unsqueeze(2).broadcast_to(wide), ALU.is_le))
                step(v.tensor_reduce(M_BF[0:1, :], M_BE[0:1, :, :], AXX, ALU.add))
                step(v.tensor_scalar(M_BF[0:1, :], M_BF[0:1, :], float(EXPERTS - 1), None, ALU.min))
                step(v.tensor_copy(BLKI[:, :], M_BF[0:1, :]))
                tell("routed")

            def moe(i):
                first = (32, 138)[i]
                norm(GAIN[:, i, 1, :], MOD[:, i, 24:32])
                for b in (1, 3):
                    empty(b, XN[:, b // 2, 512:1024])
                route()

                def turned():
                    dve.wait_ge(*nth("bank5_full_dve"))
                    tell("xr_free")
                    v.tensor_copy(XB[:, 4:8, :].rearrange("p k r -> p (k r)"), BK[5][:, :]).then_inc(bfree(5), 1)

                def block(b, last=False):
                    g = 6 if b == 0 else 0
                    th, ta, hb = (y.rearrange("p k r -> p (k r)") for y in (TH, TA, HB))
                    dve.wait_ge(*nth("tanh_ready"))
                    step(v.scalar_tensor_tensor(ta, th, 1.0, BK[g][:, :], ALU.add, ALU.mult))
                    tell(f"bank{g}_free")
                    dve.wait_ge(*nth(f"bank{g + 1}_full_dve"))
                    step(v.scalar_tensor_tensor(hb, ta, 0.5, BK[g + 1][:, :], ALU.mult, ALU.mult))
                    tell(f"bank{g + 1}_free")
                    tell("hidden_ready")
                    if not last:
                        turned()
                    dve.wait_ge(*nth(f"y{b}_stored"))
                    dve.wait_ge(*nth("bank3_full_dve"))
                    step(v.tensor_copy(YB[:, b, 512:1024], BK[3][:, :]))
                    tell(f"slot{(first + 3 * b + 2) % RING}_free")
                    tell("bank3_free")
                    tell("y_half")

                turned()
                with dve.Fori(0, NBLK // 2) as j:
                    tally.enter(j, {"dve_chain": 6, "tanh_ready": 2, "bank7_full_dve": 1, "bank1_full_dve": 1, "bank5_full_dve": 2,
                                    "bank3_full_dve": 2, "y0_stored": 1, "y1_stored": 1})
                    for b in range(2):
                        block(b)
                    tally.leave(NBLK // 2)
                block(0, last=True)
                dve.wait_ge(*nth("bank5_full_dve"))
                step(v.tensor_copy(GB[:, 512:1024], BK[5][:, :]))
                tell("bank5_free")
                dve.wait_ge(*nth("gate_spread"))
                for t in range(NT):
                    dve.wait_ge(sem[f"rows{t}_gathered"], 32 * (i + 1))
                    y1, y2 = YR[:, t, :], YR[:, NT + t, :]
                    step(v.tensor_scalar(y1, y1, M_G[:, 2, t:t + 1], None, ALU.mult))
                    step(v.scalar_tensor_tensor(y1, y2, M_G[:, 3, t:t + 1], y1, ALU.mult, ALU.add))
                    step(v.tensor_tensor(y1, y1, GB[:, :], ALU.mult))
                    step(v.tensor_tensor(X[:, t, :], X[:, t, :], y1, ALU.add))
                    tell("x_ready")

            def ffn(gain, last=False):
                split["stage"] = 0
                norm(gain, None, ahead=1, split=True)
                for j in range(NCH):
                    q, g = j % 2, 4 + 2 * (j % 2)
                    split_to(GATE_HALF[j] + SPLITS)
                    dve.wait_ge(*nth("tanh_ready"))
                    step(v.scalar_tensor_tensor(F_TA, F_TH[:, q, :], 1.0, BK[g][:, :], ALU.add, ALU.mult))
                    tell(f"bank{g}_free")
                    dve.wait_ge(*nth(f"bank{g + 1}_full_dve"))
                    step(v.scalar_tensor_tensor(F_TA, F_TA, 0.5, BK[g + 1][:, :], ALU.mult, ALU.mult))
                    tell(f"bank{g + 1}_free")
                    hi, lo = (y[:, q, :, :].rearrange("p a s -> p (a s)") for y in (F_HI, F_LO))
                    step(v.tensor_copy(hi, F_TA))
                    step(v.tensor_tensor(lo, F_TA, hi.bitcast(F32), ALU.subtract))
                    tell("hidden_ready")
                split_to(len(FFN_HALVES))
                ring[0] += FFN_SLOTS
                add_plain(0.5, last)

            def log_sigmoid(dst, src, ln):
                dve.wait_ge(*nth("ln_ready"))
                step(v.scalar_tensor_tensor(dst, src, 0.0, ln, ALU.min, ALU.subtract))

            ada_slots = {"ring": 0, "n": 0}

            def ada_slot():
                s, n = ada_slots["ring"] % RING, ada_slots["n"]
                ada_slots["ring"] += 1
                ada_slots["n"] += 1
                w = slot(s).rearrange("p (k n) -> p k n", k=KD)
                dve.wait_ge(*nth(f"slot{s}_full"))
                if n >= 2:
                    dve.wait_ge(*nth("sums_taken"))
                for k in range(KD):
                    acc = PS[:, n % 2, k % 2, :]
                    if k < 2:
                        ins = v.tensor_scalar(acc, w[:, k, :], CA[:, k:k + 1], None, ALU.mult)
                    else:
                        dve.wait_ge(*tally.behind("dve_chain", 1))
                        ins = v.scalar_tensor_tensor(acc, w[:, k, :], CA[:, k:k + 1], acc, ALU.mult, ALU.add)
                    ins.then_inc(sem["dve_chain"], 1)
                    tally.skip("dve_chain")
                dve.wait_ge(*tally.behind("dve_chain", 0))
                tell(f"slot{s}_free")
                step(v.tensor_tensor(PS[:, n % 2, 0, :], PS[:, n % 2, 0, :], PS[:, n % 2, 1, :], ALU.add))
                tell("sums_ready")

            def other_slot():
                tally.skip(f"slot{ada_slots['ring'] % RING}_full")
                ada_slots["ring"] += 1

            def modulation(b, first, last, gains):
                for s_ in range(2):
                    dve.wait_ge(*nth("sums_taken"))
                ada_slots["n"] = 0
                dve.wait_ge(*nth(f"bank{b}_full_dve"))
                step(v.tensor_tensor(MOD.rearrange("p i n -> p (i n)")[:, first:last], BK[b][:, 0:last - first],
                                     VT2[:, first:last], ALU.add))
                tell(f"bank{b}_free")
                for i, w in gains:
                    at = VEC[("norm_mix_g", "norm_ffn_g")[w]] + 8 * i
                    step(v.scalar_tensor_tensor(GAIN[:, i, w, :], MOD[:, i, 8 + 24 * w:16 + 24 * w], 1.0, VT1[:, at:at + 8],
                                                ALU.add, ALU.mult))

            empty(0, VT1[:, :], src=BK[0][:, 0:NVEC])
            empty(1, VT2[:, :], src=BK[1][:, 0:96])
            dve.wait_ge(*nth("bank2_full_dve"))
            step(v.tensor_copy(VT3[:, :], BK[2][:, 0:64]))
            tell("bank2_free")
            tell("vecs_ready")
            dve.wait_ge(*nth("tanh_ready"))
            step(v.scalar_tensor_tensor(CA[:, :], CT1[:, :], 1.0, VT1[:, 0:8], ALU.add, ALU.mult))
            step(v.tensor_scalar(CA[:, :], CA[:, :], 0.5, None, ALU.mult))
            tell("c_ready")
            for n in range(ADA_EARLY):
                ada_slot()
            dve.wait_ge(sem["smalls"], 16 * SMALLS.count("smalls"))
            for t in range(NT):
                tell("x_ready")
            modulation(3, 0, 4 * ADA_EARLY, ((0, 0),))
            tell("mod_ready")

            norm(GAIN[:, 0, 0, :], MOD[:, 0, 0:8])

            def ada_pair():
                other_slot()
                ada_slot()
                ada_slot()

            ada_pair()
            for n in (1, 3, 5, 7):
                dve.wait_ge(*nth(f"bank{n % 4}_full_dve"))
                v.tensor_scalar(QK[:, 2 * n:2 * n + 2, :].rearrange("p a s -> p (a s)"), BK[n % 4][:, :],
                                0.125 if n < 4 else 1.0, None, ALU.mult).then_inc(bfree(n % 4), 1)
                if n > 1:
                    ada_pair()
            for n in (1, 3):
                empty(n, VV[:, 1, (n // 2) * 512:(n // 2) * 512 + 512])
                if n == 1:
                    ada_pair()
            other_slot()
            modulation(6, 4 * ADA_EARLY, 4 * ADA_EARLY + 40, ((0, 1),))
            FLf, FAf, FEf, FMf, FCf = (y.rearrange("p t h -> p (t h)") for y in (FL, FA, FE, FM, FC))
            dve.wait_ge(*nth("bank4_full_dve"))
            step(v.tensor_tensor(FL, BK[4][:, 0:NT * HEADS].rearrange("p (t h) -> p t h", t=NT),
                                 FBIAS[:, :].unsqueeze(1).broadcast_to([P, NT, HEADS]), ALU.add))
            tell("bank4_free")
            step(v.scalar_tensor_tensor(FAf, FLf, -1.0, FLf, ALU.mult, ALU.max))
            tell("fa_ready")
            log_sigmoid(FMf, FLf, FEf)
            tell("logf_ready")
            dve.wait_ge(*nth("bank5_full_dve"))
            step(v.tensor_copy(FCf, BK[5][:, 0:NT * HEADS]))
            tell("bank5_free")
            tell("f_ready")
            mask = causal[:, P:2 * P].unsqueeze(1).broadcast_to([P, 4, P])
            for n in range(8):
                if n < 4:
                    dve.wait_ge(*nth("unmasked_ready"))
                    dst = NF0[:, 4 * n:4 * n + 4, :]
                else:
                    dve.wait_ge(*nth(f"bank{n}_full_dve"))
                    dst = NF1[:, 4 * (n - 4):4 * (n - 4) + 4, P:2 * P]
                step(v.scalar_tensor_tensor(dst, BK[n][:, :].rearrange("p (h s) -> p h s", h=4), -1.0, mask,
                                            ALU.mult, ALU.add))
                tell(f"bank{n}_free")

            def attend(h):
                q, b = h % 2, 4 + h % 2
                dve.wait_ge(*nth(f"bank{b}_full_dve"))
                v.scalar_tensor_tensor(LG[:, q, 0:128], BK[b][:, 0:128], FC[:, 0, h:h + 1], NF0[:, h, :], ALU.add, ALU.add)
                step(v.scalar_tensor_tensor(LG[:, q, 128:384], BK[b][:, 128:384], FC[:, 1, h:h + 1], NF1[:, h, :],
                                            ALU.add, ALU.add))
                tell(f"bank{b}_free")
                v.tensor_reduce(AMX[:, q, 0:1], LG[:, q, 0:128], AXX, ALU.max, negate=True)
                v.tensor_reduce(AMX[:, q, 1:2], LG[:, q, 128:384], AXX, ALU.max, negate=True).then_inc(sem["logits_ready"], 1)

            def weigh(h):
                q = h % 2
                dve.wait_ge(*nth("exp_ready"))
                step(v.reciprocal(ARS[:, q, :], ASM[:, q, :]))
                v.tensor_scalar(LG[:, q, 0:128], LG[:, q, 0:128], ARS[:, q, 0:1], None, ALU.mult)
                v.tensor_scalar(LG[:, q, 128:384], LG[:, q, 128:384], ARS[:, q, 1:2], None, ALU.mult)\
                    .then_inc(sem["probs_ready"], 1)

            for h in range(HEADS):
                attend(h)
                if h >= 1:
                    weigh(h - 1)
                if h >= 4 and h % 2 == 0:
                    empty(2 + (h // 2) % 2, OT[:, h // 2 - 2, :], src=BK[2 + (h // 2) % 2][:, 0:S])
                if h < 14 - ADA_EARLY:
                    ada_slot()
            modulation(0, 4 * ADA_EARLY + 40, 96, ((1, 0), (1, 1)))
            step(v.tensor_tensor(CSG[:, :], MOD[:, 1, 16:24], VT1[:, VEC["pool_scale"]:VEC["pool_scale"] + 8], ALU.mult))
            tell("mod_ready")
            weigh(HEADS - 1)
            for m in (HEADS // 2 - 2, HEADS // 2 - 1):
                empty(2 + m % 2, OT[:, m, :], src=BK[2 + m % 2][:, 0:S])
            add_gated(YT)
            moe(0)

            for y in (HP, W0, W1):
                v.memset(y[:, :, 0:16], 0.0)
            norm(GAIN[:, 1, 0, :], MOD[:, 1, 0:8], dst=HP, pad=16)
            dve.wait_ge(*nth("pool_in_ready"))
            src, dst = HP, W0
            for g, w in enumerate((2, 4, 8, 16)):
                k = 2 * g
                step(v.tensor_tensor(dst[:, k:8, 16:16 + S], src[:, k:8, 16:16 + S], src[:, k:8, 16 - w // 2:16 + S - w // 2],
                                     ALU.add))
                src, dst = dst, (W1 if dst is W0 else W0)
                ws, h = src[:, k:k + 2, 16:16 + S], HP[:, k:k + 2, 16:16 + S]
                step(v.scalar_tensor_tensor(PL[:, k:k + 2, :], ws, 1.0 / w, h, ALU.mult, ALU.subtract))
                inv = cst("inv")[:, 16 * g:16 * g + 16].unsqueeze(1).broadcast_to([P, 2, 16])
                step(v.tensor_tensor(PFIX, ws[:, :, 0:16], inv, ALU.mult))
                step(v.tensor_tensor(PL[:, k:k + 2, 0:16], PFIX, h[:, :, 0:16], ALU.subtract))
            tell("pooled_ready")
            add_gated(YT)
            moe(1)
            mean_square()
            for t in range(NT):
                dve.wait_ge(*nth("rstd_ready"))
                step(v.scalar_tensor_tensor(X[:, t, :], X[:, t, :], RSTD[:, t:t + 1], NFG[:, :], ALU.mult, ALU.mult))
                tell("x_ready")

            for l in range(2):
                ffn(VT1[:, VEC["ffn1_norm"] + 8 * l:VEC["ffn1_norm"] + 8 * l + 8])
                norm(VT1[:, VEC["mix_norm"] + 8 * l:VEC["mix_norm"] + 8 * l + 8], None)
                v.memset(CV[:, :, 0:3], 0.0)
                v.memset(VMA[:, :, :, MD:MD + 1].rearrange("p t h o -> p t (h o)"), 1.0)
                v.tensor_copy(GQ[:, 0:8, :], QN[:, l, :].unsqueeze(1).broadcast_to([P, 8, 64]))
                v.tensor_copy(GQ[:, 8:10, :], KN[:, l, :].unsqueeze(1).broadcast_to([P, 2, 64]))
                dve.wait_ge(*nth("bank4_full_dve"))
                step(v.tensor_tensor(GI, BK[4][:, 0:16].rearrange("p (t g) -> p t g", t=NT),
                                     GATEB[:, l, :].unsqueeze(1).broadcast_to([P, NT, 8]), ALU.add))
                tell("bank4_free")
                dve.wait_ge(*nth("rows_ready"))
                for t in range(NT):
                    ins = v.tensor_tensor(T1[:, t, :].rearrange("p (h d) -> p h d", h=10), RB[:, t, 0:10, :],
                                          RB[:, t, 0:10, :], ALU.mult)
                step(ins)
                step(v.tensor_reduce(RSS, T1.rearrange("p t (h d) -> p (t h) d", h=10), AXX, ALU.add))
                v.tensor_scalar(RMS, RSS, 1.0 / 64, EPS, ALU.mult, ALU.add).then_inc(sem["meansq_ready"], 1)
                dve.wait_ge(*nth("rstd_ready"))
                for t in range(NT):
                    ins = v.tensor_tensor(RB[:, t, 0:10, :], RB[:, t, 0:10, :],
                                          RRS[:, 10 * t:10 * t + 10].unsqueeze(2).broadcast_to([P, 10, 64]), ALU.mult)
                step(ins)
                for t in range(NT):
                    ins = v.tensor_tensor(RB[:, t, 0:10, :], RB[:, t, 0:10, :], GQ, ALU.mult)
                step(ins)
                for t in range(NT):
                    lo, hi = RB[:, t, :, 0:32], RB[:, t, :, 32:64]
                    cos, sin = (cst(y)[:, 32 * t:32 * t + 32].unsqueeze(1).broadcast_to([P, 16, 32]) for y in ("cos", "sin"))
                    t1, t2 = (y[:, t, 0:512].rearrange("p (h d) -> p h d", h=16) for y in (T1, T2))
                    v.tensor_tensor(t1, lo, cos, ALU.mult)
                    step(v.tensor_tensor(t2, hi, sin, ALU.mult))
                    step(v.tensor_tensor(RO[:, t, :, 0:32], t1, t2, ALU.subtract))
                    v.tensor_tensor(t1, hi, cos, ALU.mult)
                    step(v.tensor_tensor(t2, lo, sin, ALU.mult))
                    step(v.tensor_tensor(RO[:, t, :, 32:64], t1, t2, ALU.add))
                tell("rotated")
                for n in (1, 3):
                    empty(n, QT[:, 2 * n:2 * n + 2, :].rearrange("p a s -> p (a s)"))
                for tb in range(NT):
                    n = P * (tb + 1)
                    mask = causal[:, 2 * P - n:2 * P]
                    lb = LB[:, 0:n]
                    dve.wait_ge(*nth("index_ready"))
                    a, b = IW[:, 0, 0:n], IW[:, 1, 0:n]
                    for j, h in enumerate((0, 2, 1, 3)):
                        step(v.scalar_tensor_tensor(a, IR[tb][:, j, :], WI[:, tb, h:h + 1], mask if j == 0 else a,
                                                    ALU.mult, ALU.add))
                    for _ in range(TOPK // 8):
                        step(v.max(out=M8, in_=a))
                        step(v.match_replace(out=b, in_to_replace=M8, in_values=a, imm_value=GONE))
                        a, b = b, a
                    step(v.tensor_scalar(lb, a, GONE / 2, NEG, ALU.is_gt, ALU.mult))
                    step(v.tensor_tensor(lb, lb, mask, ALU.add))
                    la = LA[tb]
                    banks = (0, 1) if tb == 0 else (2, 3, 0, 1)
                    hh = AH // len(banks)
                    for m, b_ in enumerate(banks):
                        dve.wait_ge(*nth(f"bank{b_}_full_dve"))
                        step(v.scalar_tensor_tensor(la[:, hh * m:hh * m + hh, :],
                                                    BK[b_][:, :].rearrange("p (h s) -> p h s", h=hh), 0.125,
                                                    lb.unsqueeze(1).broadcast_to([P, hh, n]), ALU.mult, ALU.add))
                        tell(f"bank{b_}_free")
                    v.tensor_reduce(AM[:, tb, :], la, AXX, ALU.max, negate=True).then_inc(sem["logits_ready"], 1)
                    dve.wait_ge(*nth("exp_ready"))
                    step(v.reciprocal(AR[:, tb, :], AS[:, tb, :]))
                    v.tensor_tensor(la, la, AR[:, tb, :].unsqueeze(2).broadcast_to([P, AH, n]), ALU.mult)\
                        .then_inc(sem["probs_ready"], 1)
                convw = VT3[:, 32 * l:32 * l + 32]
                dve.wait_ge(*nth("tap_ready"))
                for tap in range(1, CONVK):
                    for k in range(KD):
                        ins = v.scalar_tensor_tensor(CO[:, k, :], CV[:, k, tap:tap + S], convw[:, 8 * tap + k:8 * tap + k + 1],
                                                     CO[:, k, :], ALU.mult, ALU.add)
                    step(ins)
                tell("conv_ready")
                f = GI[:, :, 4:8]
                LF_, LFA_, LFE_, IMB_ = (y.rearrange("p (t h) -> p t h", t=NT) for y in (LF, LFA, LFE, IMB))
                step(v.scalar_tensor_tensor(LFA_, f, -1.0, f, ALU.mult, ALU.max))
                tell("fa_ready")
                log_sigmoid(LF_, f, LFE_)
                tell("logf_ready")
                dve.wait_ge(*nth("tanh_ready"))
                step(v.scalar_tensor_tensor(CO, TH2, 1.0, CO, ALU.add, ALU.mult))
                tell("qk_ready")
                dve.wait_ge(*nth("bank7_full_dve"))
                step(v.tensor_copy(BB.rearrange("p a m -> p (a m)"), BK[7][:, 0:16]))
                tell("bank7_free")
                step(v.tensor_tensor(IMB_, GI[:, :, 0:4], BB[:, 0, :].rearrange("p (t h) -> p t h", t=NT), ALU.subtract))
                tell("imb_ready")
                for ch in range(NT):
                    b = 5 + ch
                    rows = BK[b][:, :].rearrange("p (h s) -> p h s", h=MH)
                    dve.wait_ge(*nth(f"bank{b}_full_dve"))
                    if ch == 0:
                        v.tensor_reduce(MXI, rows, AXX, ALU.max)
                    step(v.tensor_tensor(DM[:, MH * ch:MH * ch + MH, :], rows,
                                         causal[:, P:2 * P].unsqueeze(1).broadcast_to([P, MH, P]), ALU.add))
                    tell(f"bank{b}_free")
                step(v.tensor_reduce(DMX, DM, AXX, ALU.max))
                last = BB[:, 1, 0:MH]
                step(v.tensor_tensor(AMAX, last, MXI, ALU.add))
                step(v.tensor_tensor(M1_, last, AMAX, ALU.max))
                v.tensor_copy(GG[:, 0:MH], BB[:, 0, 0:MH])
                step(v.tensor_tensor(GG[:, MH:8], BB[:, 0, MH:8], M1_, ALU.add))
                step(v.tensor_tensor(MTT, BB[:, 0, :], DMX, ALU.add))
                step(v.tensor_tensor(MTT, MTT, GG, ALU.max))
                v.tensor_tensor(BMT, BB[:, 0, :], MTT, ALU.subtract)
                v.tensor_tensor(EX[:, 0:8], GG, MTT, ALU.subtract)
                v.tensor_scalar(EX[:, 8:16], MTT, -1.0, None, ALU.mult)
                v.tensor_tensor(EX[:, 16:20], IMB[:, 0:MH], MXI, ALU.subtract)
                v.tensor_tensor(EX[:, 20:24], AMAX, M1_, ALU.subtract).then_inc(sem["exponents_ready"], 1)
                dve.wait_ge(*nth("exp_ready"))
                kd = float(MD) ** -0.5
                v.tensor_scalar(WIH[:, 0:MH], EO[:, 4:8], 0.5, None, ALU.mult)
                step(v.scalar_tensor_tensor(KWS[:, 0:MH], EO[:, 16:20], 0.5 * kd, EO[:, 20:24], ALU.mult, ALU.mult))
                for ch in range(NT):
                    dve.wait_ge(*nth(f"bank{ch}_full_dve"))
                    part = DM[:, MH * ch:MH * ch + MH, :]
                    step(v.scalar_tensor_tensor(part, BK[ch][:, :].rearrange("p (h s) -> p h s", h=MH), 0.25 * kd, part,
                                                ALU.mult, ALU.mult))
                    tell(f"bank{ch}_free")
                tell("weighted_ready")
                step(v.tensor_reduce(SSUM, DM, AXX, ALU.add))
                dve.wait_ge(*nth("bank2_full_dve"))
                for h in range(MH):
                    ins = v.tensor_scalar(KW[:, h, :], BK[2][:, P * h:P * h + P], KWS[:, h:h + 1], None, ALU.mult)
                step(ins)
                tell("bank2_free")
                tell("keys_ready")
                for m, b in enumerate((7, 2)):
                    dve.wait_ge(*nth(f"bank{b}_full_dve"))
                    for i in range(2):
                        h = 2 * m + i
                        ins = v.tensor_scalar(IN[:, h, :], BK[b][:, 129 * i:129 * i + 129], WIH[:, h:h + 1], None, ALU.mult)
                    step(ins)
                    tell(f"bank{b}_free")
                v.tensor_copy(DEN[:, 0:MH], SSUM[:, 0:MH])
                step(v.tensor_tensor(DEN[:, MH:8], SSUM[:, MH:8], IN[:, :, MD], ALU.add))
                step(v.scalar_tensor_tensor(DEN, DEN, -1.0, DEN, ALU.mult, ALU.max))
                step(v.tensor_tensor(DEN, DEN, EO[:, 8:16], ALU.max))
                step(v.reciprocal(RDEN, DEN))
                for ch in range(NT):
                    part = HN[:, MH * ch:MH * ch + MH, :]
                    rows = BK[ch][:, :].rearrange("p (h d) -> p h d", h=MH)
                    rden = RDEN[:, MH * ch:MH * ch + MH].unsqueeze(2).broadcast_to([P, MH, MD])
                    dve.wait_ge(*nth(f"bank{ch}_full_dve"))
                    if ch == 0:
                        step(v.tensor_tensor(part, rows, rden, ALU.mult))
                        tell("bank0_free")
                    else:
                        step(v.tensor_tensor(part, rows, IN[:, :, 0:MD], ALU.add))
                        tell("bank1_free")
                        step(v.tensor_tensor(part, part, rden, ALU.mult))
                step(v.tensor_tensor(HQ, HN, HN, ALU.mult))
                step(v.tensor_reduce(HSS, HQ, AXX, ALU.add))
                v.tensor_scalar(HMS, HSS, 1.0 / MD, EPS, ALU.mult, ALU.add).then_inc(sem["meansq_ready"], 1)
                dve.wait_ge(*nth("rstd_ready"))
                step(v.tensor_tensor(HN, HN, HRS.unsqueeze(2).broadcast_to([P, 8, MD]), ALU.mult))
                hn = HN.rearrange("p (c h) d -> p c (h d)", c=NT)
                for ch in range(NT):
                    ins = v.scalar_tensor_tensor(hn[:, ch, :], hn[:, ch, :], 0.5, MN[:, l, :], ALU.mult, ALU.mult)
                step(ins)
                step(v.scalar_tensor_tensor(hn, OG, 1.0, hn, ALU.add, ALU.mult))
                tell("mlstm_ready")
                add_plain(1.0)
                ring[0] += 6 + 2
                ffn(VT1[:, VEC["ffn2_norm"] + 8 * l:VEC["ffn2_norm"] + 8 * l + 8], last=l == 1)

        @block.tensor
        def _(pe):
            tally = Tally(sem)
            nth, peek = tally.nth, tally.peek
            ring = [0]
            used = []

            def mm(*args, **kw):
                ins = nc.tensor.matmul(*args, **kw)
                if used:
                    ins.then_inc(sem[used.pop(0)], 1)
                return ins

            def turn(dst, src):
                return mm(dst, src, ident[0:src.shape[0], 0:src.shape[0]], is_transpose=True)

            def fill(b):
                pe.wait_ge(*nth(f"bank{b}_free"))

            def emptied(*banks):
                for b in banks:
                    pe.wait_ge(*peek(f"bank{b}_free"))

            def arrived(parts=1):
                s = ring[0] % RING
                ring[0] += 1
                for _ in range(parts):
                    at = nth(f"slot{s}_full")
                pe.wait_ge(*at)
                return s, slot(s)

            def norm():
                for t in range(NT):
                    pe.wait_ge(*nth("xn_ready"))
                    for b in range(4, 8):
                        if t == 0:
                            fill(b)
                        for j in range(2):
                            k = 2 * (b - 4) + j
                            ins = turn(BK[b][:, j * S + t * P:j * S + t * P + P], XN[:, t, k * P:(k + 1) * P])
                        if t == NT - 1:
                            ins.then_inc(bfull(b, "dve" if b % 2 else "act"), 1)

            def spread_gate(col):
                for b in (4, 5):
                    fill(b)
                    for j in range(4):
                        k = 4 * (b - 4) + j
                        ins = mm(BK[b][:, j * P:(j + 1) * P], bcol(col[:, k:k + 1]), ident, start=True, stop=True)
                    ins.then_inc(bfull(b, "dve" if b % 2 else "act"), 1)

            def project(src):
                for h in range(2):
                    s, w = arrived()
                    w = w.rearrange("p (k n) -> p k n", k=KD)
                    for t in range(NT):
                        b = 2 * t + h
                        fill(b)
                        for k in range(KD):
                            ins = mm(BK[b][:, :], src[:, k, t * P:(t + 1) * P], w[:, k, :], start=k == 0, stop=k == KD - 1)
                        ins.then_inc(bfull(b, "dve"), 1)
                    used.append(f"slot{s}_free")

            def ada_slot(b, c):
                pe.wait_ge(*nth("sums_ready"))
                for j in range(4):
                    ins = mm(BK[b][:, 4 * c + j:4 * c + j + 1], PS[:, c % 2, 0, j * P:(j + 1) * P], cst("ones")[:, 0:1],
                             start=True, stop=True)
                ins.then_inc(sem["sums_taken"], 1)

            def other_slots(n):
                for _ in range(n):
                    tally.skip(f"slot{ring[0] % RING}_full")
                    ring[0] += 1

            def close_ada(b):
                mm(BK[b][:, 48:49], ident, cst("ones")[:, 0:1], start=True, stop=True).then_inc(bfull(b, "dve"), 1)

            def moe():
                norm()
                emptied(4, 5, 6, 7)
                for b in range(4):
                    t, h = b // 2, b % 2
                    fill(b)
                    for j in range(4):
                        ins = turn(BK[b][:, j * P:(j + 1) * P], HT[:, 4 * h + j, t * P:(t + 1) * P])
                    ins.then_inc(bfull(b, "dve" if b % 2 else "act"), 1)
                fill(4)
                for t in range(NT):
                    for k in range(KD):
                        ins = mm(BK[4][:, t * EXPERTS:(t + 1) * EXPERTS], HT[:, k, t * P:(t + 1) * P], WR[:, k, :],
                                 start=k == 0, stop=k == KD - 1)
                ins.then_inc(bfull(4, "act"), 1)
                pe.wait_ge(*nth("choice_ready"))
                fill(5)
                E = EXPERTS
                mm(BK[5][:, 0:E], cst("before"), M_A[:, 0, :], start=True, stop=True)
                mm(BK[5][:, E:2 * E], cst("before"), M_A[:, 1, :], start=True, stop=False)
                mm(BK[5][:, E:2 * E], cst("ones"), M_A[:, 0, :], start=False, stop=True)
                mm(BK[5][:, 2 * E:3 * E], cst("ones"), M_A[:, 0, :], start=True, stop=False)
                mm(BK[5][:, 2 * E:3 * E], cst("ones"), M_A[:, 1, :], start=False, stop=True).then_inc(bfull(5, "dve"), 1)

                def turn_rows(b):
                    pe.wait_ge(*nth(f"xr{b}_full"))
                    for bank in (4, 5):
                        fill(bank)
                        for j in range(4):
                            k = 4 * (bank - 4) + j
                            ins = turn(BK[bank][:, j * ROWS:(j + 1) * ROWS], XR[:, b, k * P:(k + 1) * P])
                        ins.then_inc(bfull(bank, "dve" if bank % 2 else "act"), 1)

                def block(b, last=False):
                    emptied(4, 5)
                    for bank in (6, 7) if b == 0 else (0, 1):
                        fill(bank)
                        s, w = arrived()
                        w = w.rearrange("p (k n) -> p k n", k=KD)
                        for m in range(4):
                            for k in range(KD):
                                ins = mm(BK[bank][:, m * ROWS:(m + 1) * ROWS], w[:, k, m * P:(m + 1) * P], XB[:, k, :],
                                         start=k == 0, stop=k == KD - 1)
                        ins.then_inc(bfull(bank, "dve" if bank % 2 else "act"), 1)
                        used.append(f"slot{s}_free")
                    if not last:
                        turn_rows((b + 1) % 2)
                    pe.wait_ge(*nth("hidden_ready"))
                    s, w = arrived()
                    w = w.rearrange("p (k n) -> p k n", k=4)
                    for h in range(2):
                        fill(2 + h)
                        for k in range(4):
                            ins = mm(BK[2 + h][:, :], HB[:, k, :], w[:, k, h * 512:(h + 1) * 512], start=k == 0, stop=k == 3)
                        ins.then_inc(bfull(2 + h, "dve" if h else "act"), 1)

                turn_rows(0)
                with pe.Fori(0, NBLK // 2) as j:
                    tally.enter(j, {"hidden_ready": 2, "bank4_free": 2, "bank5_free": 2, "bank6_free": 1, "bank7_free": 1,
                                    "bank0_free": 1, "bank1_free": 1, "bank2_free": 2, "bank3_free": 2, "xr0_full": 1, "xr1_full": 1}
                                | {f"slot{s}_full": 1 for s in range(RING)})
                    for b in range(2):
                        block(b)
                    tally.leave(NBLK // 2)
                block(0, last=True)

            halves = [0]

            def product(dst, a, b, start, stop):
                mm(dst, a[0], b[0], start=start, stop=False)
                mm(dst, a[0], b[1], start=False, stop=False)
                return mm(dst, a[1], b[0], start=False, stop=stop)

            def ffn():
                norm()
                first = ring[0]
                ring[0] += FFN_SLOTS
                for at in range(FFN_SLOTS):
                    for _ in range(2 if at % 3 != 2 and at < FFN_SLOTS - 1 else 1):
                        tally.skip(f"slot{(first + at) % RING}_full")
                pe.wait_ge(*nth("h_lo_ready"))
                todo = list(FFN_HALVES)

                def half():
                    at, i, _ = todo.pop(0)
                    s = (first + at) % RING
                    hi = W_HI[:, halves[0] % SPLITS, :]
                    halves[0] += 1
                    pe.wait_ge(*nth("w_lo_ready"))
                    out = ["w_hi_free"]
                    if at not in [a for a, *_ in todo]:
                        out.append(f"slot{s}_free")
                    return out, (hi, SLOTS[s][1][:, i * HALF:(i + 1) * HALF])

                for what, j in FFN_STEPS:
                    if what == "up":
                        for a in range(2):
                            b = 4 + 2 * (j % 2) + a
                            done, w = half()
                            w = [y.rearrange("p (k n) -> p k n", k=KD) for y in w]
                            fill(b)
                            for m in range(2):
                                for k in range(KD):
                                    if (j, a, m, k) == (0, 0, 0, KD // 2):
                                        pe.wait_ge(*nth("h_lo_ready"))
                                    ins = product(BK[b][:, m * S:(m + 1) * S], [y[:, k, m * P:(m + 1) * P] for y in w],
                                                  (HT_HI[:, k, :], HT_LO[:, k, :]), start=k == 0, stop=k == KD - 1)
                            ins.then_inc(bfull(b, "dve" if a else "act"), 1)
                            used.extend(done)
                    else:
                        done, w = half()
                        w = [y.rearrange("p (k n) -> p k n", k=2) for y in w]
                        pe.wait_ge(*nth("hidden_ready"))
                        for b in range(4):
                            t, h = b // 2, b % 2
                            if j == 0:
                                fill(b)
                            for i in range(2):
                                ins = product(BK[b][:, :], [y[:, j % 2, i, t * P:(t + 1) * P] for y in (F_HI, F_LO)],
                                              [y[:, i, h * 512:(h + 1) * 512] for y in w],
                                              start=j == 0 and i == 0, stop=j == NCH - 1 and i == 1)
                            if j == NCH - 1:
                                ins.then_inc(bfull(b, "dve"), 1)
                        used.extend(done)

            pe.wait_ge(sem["vectors"], 16 * SMALLS.count("vectors"))
            for b, n in ((0, NVEC), (1, 96), (2, 64)):
                fill(b)
                turn(BK[b][:, 0:n], VR[0:n, b, :]).then_inc(bfull(b, "dve"), 1)
            pe.wait_ge(*nth("c_ready"))
            fill(3)
            for c in range(ADA_EARLY):
                ada_slot(3, c)
            other_slots(ADA_EARLY)
            close_ada(3)

            norm()
            emptied(4, 5, 6, 7)
            fill(6)

            def ada_sums(pair):
                for c in (2 * pair, 2 * pair + 1):
                    ada_slot(6, c)

            for n in range(8):
                if n % 2 == 0:
                    if n:
                        other_slots(2)
                    s, w = arrived()
                    w = w.rearrange("p (k n) -> p k n", k=KD)
                b = n % 4
                fill(b)
                for i in range(2):
                    m = 2 * (n % 2) + i
                    for k in range(KD):
                        ins = mm(BK[b][:, i * S:(i + 1) * S], w[:, k, m * P:(m + 1) * P], HT[:, k, :],
                                 start=k == 0, stop=k == KD - 1)
                ins.then_inc(bfull(b, "dve" if n % 2 else "act"), 1)
                if n % 2 == 1:
                    used.append(f"slot{s}_free")
                    if n > 1:
                        ada_sums(n // 2 - 1)
            for h in range(2):
                other_slots(2)
                s, w = arrived()
                w = w.rearrange("p (k n) -> p k n", k=KD)
                for t in range(NT):
                    b = 2 * h + t
                    fill(b)
                    for k in range(KD):
                        ins = mm(BK[b][:, :], HT[:, k, t * P:(t + 1) * P], w[:, k, :], start=k == 0, stop=k == KD - 1)
                    ins.then_inc(bfull(b, "dve" if t else "act"), 1)
                used.append(f"slot{s}_free")
                ada_sums(3 + h)
            close_ada(6)
            fill(4)
            for t in range(NT):
                for k in range(KD):
                    ins = mm(BK[4][:, t * HEADS:(t + 1) * HEADS], HT[:, k, t * P:(t + 1) * P], WF[:, k, :],
                             start=k == 0, stop=k == KD - 1)
            ins.then_inc(bfull(4, "dve"), 1)
            pe.wait_ge(*nth("logf_ready"))
            fill(5)
            mm(BK[5][:, 0:HEADS], cst("upto"), FM[:, 0, :], start=True, stop=True)
            mm(BK[5][:, HEADS:2 * HEADS], cst("upto"), FM[:, 1, :], start=True, stop=False)
            mm(BK[5][:, HEADS:2 * HEADS], cst("ones"), FM[:, 0, :], start=False, stop=True).then_inc(bfull(5, "dve"), 1)
            pe.wait_ge(*nth("f_ready"))
            for n in range(8):
                fill(n)
                for j in range(4):
                    h = 4 * (n % 4) + j
                    ins = mm(BK[n][:, j * P:(j + 1) * P], bcol(FC[:, n // 4, h:h + 1]), ident, start=True, stop=True)
                ins.then_inc(bfull(n, "act" if n < 4 else "dve"), 1)

            def scores(h):
                b, at, m = 4 + h % 2, 64 * (h % 2), h // 2
                q, k = QK[at:at + 64, m, :], QK[at:at + 64, 8 + m, :]
                fill(b)
                mm(BK[b][:, 0:P], q[:, 0:P], k[:, 0:P], start=True, stop=True)
                mm(BK[b][:, P:3 * P], q[:, P:2 * P], k[:, :], start=True, stop=True).then_inc(bfull(b, "dve"), 1)

            def turn_probs(h):
                b = 6 + h % 2
                pe.wait_ge(*nth("probs_ready"))
                fill(b)
                for j in range(3):
                    ins = turn(BK[b][:, j * P:(j + 1) * P], LG[:, h % 2, j * P:(j + 1) * P])
                ins.then_inc(bfull(b, "act"), 1)

            def values(h):
                m, at = h // 2, 64 * (h % 2)
                b = 2 + m % 2
                if h % 2 == 0:
                    fill(b)
                emptied(6 + h % 2)
                o, pt = BK[b][at:at + 64, 0:S], PT[:, h % 2, :]
                mm(o, VV[:, 0, h * 64:h * 64 + 64], pt[:, 0:S], start=True, stop=False, skip_group_check=True)
                ins = mm(o[:, P:S], VV[:, 1, h * 64:h * 64 + 64], pt[:, S:S + P], start=False, stop=True,
                         skip_group_check=True)
                if h % 2 == 1:
                    ins.then_inc(bfull(b, "dve"), 1)

            for h in range(HEADS):
                scores(h)
                if h >= 1:
                    turn_probs(h - 1)
                if h >= 2:
                    values(h - 2)
                if h == 1:
                    fill(0)
                if 1 <= h < 15 - ADA_EARLY:
                    ada_slot(0, h - 1)
            other_slots(14 - ADA_EARLY)
            close_ada(0)
            turn_probs(HEADS - 1)
            values(HEADS - 2)
            values(HEADS - 1)
            spread_gate(MOD[:, 0, 16:24])
            emptied(2, 3)
            project(OT)
            moe()
            spread_gate(MOD[:, 0, 40:48])

            norm()
            pe.wait_ge(*nth("pooled_ready"))
            spread_gate(CSG[:, :])
            s, w = arrived()
            w = w[:, 0:2048].rearrange("p (a n) -> p a n", a=8)
            for b in range(4):
                t, h = b // 2, b % 2
                fill(b)
                for i in range(2):
                    g = 2 * h + i
                    for k in range(2):
                        ins = mm(BK[b][:, i * 256:(i + 1) * 256], PL[:, 2 * g + k, t * P:(t + 1) * P], w[:, 2 * g + k, :],
                                 start=k == 0, stop=k == 1)
                ins.then_inc(bfull(b, "dve"), 1)
            used.append(f"slot{s}_free")
            moe()
            spread_gate(MOD[:, 1, 40:48])

            for l in range(2):
                ffn()
                norm()
                emptied(4, 5, 6, 7)

                def before_conv(b0):
                    s, w = arrived()
                    w = w.rearrange("p (k n) -> p k n", k=KD)
                    for b in (b0, b0 + 1):
                        fill(b)
                        for i in range(2):
                            m = 2 * (b - b0) + i
                            for k in range(KD):
                                ins = mm(BK[b][:, i * S:(i + 1) * S], w[:, k, m * P:(m + 1) * P], HT[:, k, :],
                                         start=k == 0, stop=k == KD - 1)
                        ins.then_inc(bfull(b, "act"), 1)
                    used.append(f"slot{s}_free")

                def rows(b0, cols=512):
                    s, w = arrived()
                    w = w[:, 0:KD * cols].rearrange("p (k n) -> p k n", k=KD)
                    for t in range(NT):
                        fill(b0 + t)
                        for k in range(KD):
                            ins = mm(BK[b0 + t][:, 0:cols], HT[:, k, t * P:(t + 1) * P], w[:, k, :],
                                     start=k == 0, stop=k == KD - 1)
                        ins.then_inc(bfull(b0 + t, "act"), 1)
                    used.append(f"slot{s}_free")

                rows(4)
                rows(6, C_QKM - C_K)
                fill(4)
                for t in range(NT):
                    for k in range(KD):
                        ins = mm(BK[4][:, 8 * t:8 * t + 8], HT[:, k, t * P:(t + 1) * P], WIF[:, l, k, :],
                                 start=k == 0, stop=k == KD - 1)
                ins.then_inc(bfull(4, "dve"), 1)
                before_conv(0)
                pe.wait_ge(*nth("rotated"))
                for n in range(4):
                    fill(n)
                    for j in range(2):
                        for t in range(NT):
                            src = RO[:, t, 4 * n + 2 * j:4 * n + 2 * j + 2, :].rearrange("p h d -> p (h d)")
                            ins = turn(BK[n][:, j * S + t * P:j * S + t * P + P], src)
                    ins.then_inc(bfull(n, "dve" if n % 2 else "act"), 1)
                emptied(0, 1, 2, 3)

                def dots(b, q_pairs, k_pair, tb, heads):
                    n = P * (tb + 1)
                    fill(b)
                    for j, h in enumerate(heads):
                        at = 64 * (h % 2)
                        if j and h % 2 != heads[j - 1] % 2:
                            ins.then_inc(sem["pe_chain"], 1)
                            pe.wait_ge(*nth("pe_chain"))
                        ins = mm(BK[b][:, j * n:(j + 1) * n], QT[at:at + 64, q_pairs + h // 2, tb * P:(tb + 1) * P],
                                 QT[at:at + 64, k_pair, 0:n], start=True, stop=True)
                    return ins

                dots(4, 5, 7, 0, (0, 2, 1, 3)).then_inc(bfull(4, "act"), 1)
                dots(5, 5, 7, 1, (0, 2)).then_inc(bfull(5, "act"), 1)
                dots(6, 5, 7, 1, (1, 3)).then_inc(bfull(6, "act"), 1)
                order = (0, 2, 4, 6, 1, 3, 5, 7)
                for m in range(2):
                    dots(m, 0, 4, 0, order[4 * m:4 * m + 4]).then_inc(bfull(m, "dve"), 1)
                for m, b in enumerate((2, 3, 0, 1)):
                    if m == 2:
                        before_conv(4)
                    dots(b, 0, 4, 1, order[2 * m:2 * m + 2]).then_inc(bfull(b, "dve"), 1)
                rows(6)
                rows(4)
                for tb in range(NT):
                    pe.wait_ge(*nth("probs_ready"))
                    for b, h0, kt in (((4, 0, 0), (5, 4, 0)) if tb == 0 else ((6, 0, 0), (7, 4, 0), (4, 0, 1), (5, 4, 1))):
                        fill(b)
                        for j in range(4):
                            ins = turn(BK[b][:, j * P:(j + 1) * P], LA[tb][:, h0 + j, kt * P:(kt + 1) * P])
                        ins.then_inc(bfull(b, "act"), 1)
                emptied(4, 5, 6, 7)
                for m in range(AH // 2):
                    b = m // 2
                    if m % 2 == 0:
                        fill(b)
                    for i in range(2):
                        h = 2 * m + i
                        o = BK[b][64 * i:64 * i + 64, (m % 2) * S:(m % 2) * S + S]
                        h = order.index(h)
                        mm(o, VA[:, 0, :], PT0[:, h, :], start=True, stop=False, skip_group_check=True)
                        ins = mm(o[:, P:S], VA[:, 1, :], PT1[:, h, :], start=False, stop=True, skip_group_check=True)
                    if m % 2 == 1:
                        ins.then_inc(bfull(b, "act"), 1)
                pe.wait_ge(*nth("logf_ready"))
                fill(7)
                mm(BK[7][:, 0:8], cst("upto"), LF, start=True, stop=True)
                mm(BK[7][:, 8:16], cst("ones"), LF, start=True, stop=True).then_inc(bfull(7, "dve"), 1)
                pe.wait_ge(*nth("qk_ready"))
                for ch in range(NT):
                    at = slice(ch * P, (ch + 1) * P)
                    fill(ch)
                    for h in range(MH):
                        ins = mm(BK[ch][:, h * P:(h + 1) * P], CO[:, h, at], CO[:, MH + h, at], start=True, stop=True)
                    ins.then_inc(bfull(ch, "dve"), 1)
                fill(2)
                for h in range(MH):
                    ins = turn(BK[2][:, h * P:(h + 1) * P], CO[:, MH + h, 0:P])
                ins.then_inc(bfull(2, "dve"), 1)
                pe.wait_ge(*nth("imb_ready"))
                for ch in range(NT):
                    fill(5 + ch)
                    for h in range(MH):
                        ins = mm(BK[5 + ch][:, h * P:(h + 1) * P], bcol(IMB[:, MH * ch + h:MH * ch + h + 1]), ident,
                                 start=True, stop=True)
                    ins.then_inc(bfull(5 + ch, "dve"), 1)
                pe.wait_ge(*nth("weighted_ready"))
                for ch in range(NT):
                    fill(3 + ch)
                    for h in range(MH):
                        ins = turn(BK[3 + ch][:, h * P:(h + 1) * P], DM[:, MH * ch + h, :])
                    ins.then_inc(bfull(3 + ch, "act"), 1)
                pe.wait_ge(*nth("keys_ready"))
                for m in range(2):
                    fill(5 + m)
                    for i in range(2):
                        h = 2 * m + i
                        ins = mm(BK[5 + m][:, 129 * i:129 * i + 129], KW[:, h, :], VMA[:, 0, h, :], start=True, stop=True)
                    ins.then_inc(bfull(5 + m, "act"), 1)
                emptied(5, 6)
                for m, b in enumerate((7, 2)):
                    fill(b)
                    for i in range(2):
                        h = 2 * m + i
                        ins = mm(BK[b][:, 129 * i:129 * i + 129], CO[:, h, P:2 * P], CS[:, h, :], start=True, stop=True)
                    ins.then_inc(bfull(b, "dve"), 1)
                emptied(3, 4)
                for ch in range(NT):
                    fill(ch)
                    for h in range(MH):
                        ins = mm(BK[ch][:, h * P:(h + 1) * P], ST[:, MH * ch + h, :], VMA[:, ch, h, 0:MD], start=True, stop=True)
                    ins.then_inc(bfull(ch, "dve"), 1)
                w_out = []
                for h in range(2):
                    s, w = arrived()
                    w_out.append((s, w.rearrange("p (k n) -> p k n", k=KD)))

                def project_half(b, half):
                    t, h = b // 2, b % 2
                    for k in range(half * KD // 2, (half + 1) * KD // 2):
                        ins = mm(BK[b][:, :], MT[:, k, t * P:(t + 1) * P], w_out[h][1][:, k, :], start=k == 0,
                                 stop=k == KD - 1)
                    return ins

                for b in (2, 3, 0, 1):
                    fill(b)
                    project_half(b, 0)
                pe.wait_ge(*nth("mlstm_ready"))
                for m in range(2):
                    fill(4 + m)
                    for i in range(2):
                        h = 2 * m + i
                        for ch in range(NT):
                            ins = turn(BK[4 + m][:, i * S + ch * P:i * S + ch * P + P], HN[:, MH * ch + h, :])
                    ins.then_inc(bfull(4 + m, "act"), 1)
                emptied(4, 5)
                for b in range(4):
                    project_half(b, 1).then_inc(bfull(b, "dve"), 1)
                    if b >= 2:
                        used.append(f"slot{w_out[b % 2][0]}_free")
                ffn()


_INS = ["x", "c", "norm_mix_g", "norm_ffn_g", "ada_w", "ada_b", "attn_w_in", "attn_f_bias", "attn_w_o", "pool_w",
        "pool_scale", "router_w", "router_bias", "exp_w1", "exp_w3", "exp_w2", "norm_final_g", "ffn1_norm_2",
        "ffn1_w_gate_2", "ffn1_w_up_2", "ffn1_w_down_2", "mix_norm_2", "w_in_2", "conv_w_2", "conv_b_2", "gate_b_2",
        "q_norm_2", "k_norm_2", "m_norm_2", "w_out_2", "ffn2_norm_2", "ffn2_w_gate_2", "ffn2_w_up_2", "ffn2_w_down_2"]


def kernel(**inputs):
    import numpy as _np
    import concourse.bacc as _bacc
    from concourse.bass_utils import run_bass_kernel_spmd as _run

    nc = _bacc.Bacc("TRN2", target_bir_lowering=False, num_devices=1)
    arrays, args = {}, {}

    def given(name, a):
        arrays[f"in_{name}"] = a
        return nc.dram_tensor(f"in_{name}", a.shape, mybir.dt.from_np(a.dtype), kind="ExternalInput").ap()

    for name in _INS:
        args[name.removesuffix("_2")] = given(name, _np.ascontiguousarray(inputs[name]))
    consts = given("constants", constants())
    out = nc.dram_tensor("out_0", (1, S, D), F32, kind="ExternalOutput").ap()
    build(nc, args, consts, out)
    r = _run(nc, [arrays], core_ids=[0])
    return r.results[0]["out_0"]
```
